# Optimizing a Trainium2 kernel written in Bass

```python
import jax, jax.numpy as jnp
from jax import lax
import numpy as np

D_MODEL = 1024
BATCH = 1
SEQ = 1024
DEPTH = 1

RET_HEADS = 4
RET_DK = 128
RET_DV = 256
RET_CHUNK = 128
RET_QK = RET_HEADS * RET_DK
RET_V = RET_HEADS * RET_DV
ROPE_BASE = 10000.0
CONV_WIDTH = 1024
CONV_K = 3
IN_SPLITS = (RET_QK, RET_QK, RET_V, RET_V, CONV_WIDTH, CONV_WIDTH, CONV_WIDTH, D_MODEL, D_MODEL)
IN_WIDTH = 2 * RET_QK + 2 * RET_V + 3 * CONV_WIDTH + 2 * D_MODEL
PEER_HEADS = 8
PEER_NKEYS = 128
PEER_NEXPERTS = PEER_NKEYS * PEER_NKEYS
PEER_QDIM = 256
PEER_HALF = PEER_QDIM // 2
PEER_TOPK = 16
PEER_TOK_BLOCK = 128
PLE_DIM = 256
EPS = 1e-6

kernel_name = "hybrid_retention_shortconv_peer_block"

def rms_norm(x, g):
    xf = x.astype(jnp.float32)
    y = xf * lax.rsqrt(jnp.mean(xf * xf, axis=-1, keepdims=True) + EPS)
    return (y * g.astype(jnp.float32)).astype(x.dtype)

def rotary(x):
    s, half = x.shape[1], x.shape[-1] // 2
    inv = ROPE_BASE ** (-jnp.arange(half, dtype=jnp.float32) / half)
    ang = jnp.arange(s, dtype=jnp.float32)[:, None] * inv[None, :]
    cos = jnp.cos(ang)[None, :, None, :]
    sin = jnp.sin(ang)[None, :, None, :]
    x1, x2 = x[..., :half], x[..., half:]
    out = jnp.concatenate([x1 * cos - x2 * sin, x1 * sin + x2 * cos], axis=-1)
    return out.astype(x.dtype)

def chunkwise_retention(q, k, v):
    b, s, h, dk = q.shape
    dv = v.shape[-1]
    c = RET_CHUNK
    n = s // c
    log_gamma = jnp.log1p(-(2.0 ** (-5.0 - jnp.arange(h, dtype=jnp.float32))))
    pos = jnp.arange(c, dtype=jnp.float32)
    diff = pos[:, None] - pos[None, :]
    causal = diff >= 0
    decay = jnp.where(causal[None], jnp.exp(log_gamma[:, None, None] * jnp.where(causal, diff, 0.0)[None]), 0.0)
    xi = jnp.exp(log_gamma[:, None] * (pos[None, :] + 1.0))
    zeta = jnp.exp(log_gamma[:, None] * (c - 1.0 - pos[None, :]))
    chunk_decay = jnp.exp(log_gamma * c)
    qc = q.reshape(b, n, c, h, dk)
    kc = k.reshape(b, n, c, h, dk)
    vc = v.reshape(b, n, c, h, dv)
    scores = jnp.einsum('bnihd,bnjhd->bnhij', qc, kc).astype(jnp.float32) * decay[None, None]
    intra = jnp.einsum('bnhij,bnjhe->bnihe', scores, vc.astype(jnp.float32))
    kv = jnp.einsum('bnjhd,hj,bnjhe->bnhde', kc.astype(jnp.float32), zeta, vc.astype(jnp.float32))

    def step(state, kv_n):
        return state * chunk_decay[None, :, None, None] + kv_n, state

    init = jnp.zeros((b, h, dk, dv), jnp.float32)
    _, prev = lax.scan(step, init, jnp.moveaxis(kv, 1, 0))
    prev = jnp.moveaxis(prev, 0, 1)
    cross = jnp.einsum('bnihd,hi,bnhde->bnihe', qc.astype(jnp.float32), xi, prev)
    return (intra + cross).reshape(b, s, h, dv)

def head_group_norm(y):
    mu = jnp.mean(y, axis=-1, keepdims=True)
    yc = y - mu
    return yc * lax.rsqrt(jnp.mean(yc * yc, axis=-1, keepdims=True) + EPS)

def causal_short_conv(z, w, bias):
    width = z.shape[-1]
    y = lax.conv_general_dilated(z, w[:, None, :].astype(z.dtype), window_strides=(1,),
                                 padding=[(CONV_K - 1, 0)],
                                 dimension_numbers=('NWC', 'WIO', 'NWC'),
                                 feature_group_count=width)
    return y + bias.astype(z.dtype)

def peer_ffn(a, w_q, k1, k2, u, v):
    b, s, d = a.shape
    t = b * s
    af = a.reshape(t, d)
    q = (af @ w_q).reshape(t, PEER_HEADS, 2, PEER_HALF)
    s1 = jnp.einsum('thd,hnd->thn', q[:, :, 0], k1).astype(jnp.float32)
    s2 = jnp.einsum('thd,hnd->thn', q[:, :, 1], k2).astype(jnp.float32)
    v1, i1 = lax.top_k(s1, PEER_TOPK)
    v2, i2 = lax.top_k(s2, PEER_TOPK)
    cand_s = (v1[..., :, None] + v2[..., None, :]).reshape(t, PEER_HEADS, PEER_TOPK * PEER_TOPK)
    cand_i = (i1[..., :, None] * PEER_NKEYS + i2[..., None, :]).reshape(t, PEER_HEADS, PEER_TOPK * PEER_TOPK)
    top_s, top_pos = lax.top_k(cand_s, PEER_TOPK)
    idx = jnp.take_along_axis(cand_i, top_pos, axis=-1)
    gate = jax.nn.softmax(top_s, axis=-1)
    n_sel = PEER_HEADS * PEER_TOPK
    nb = t // PEER_TOK_BLOCK
    idx = idx.reshape(nb, PEER_TOK_BLOCK, n_sel)
    gate = gate.reshape(nb, PEER_TOK_BLOCK, n_sel)
    xb_all = af.reshape(nb, PEER_TOK_BLOCK, d)

    def block(args):
        xb, ib, gb = args
        ue = jnp.take(u, ib, axis=0)
        act = jax.nn.gelu(jnp.einsum('td,ted->te', xb, ue).astype(jnp.float32), approximate=False)
        ve = jnp.take(v, ib, axis=0)
        return jnp.einsum('te,ted->td', (gb * act).astype(xb.dtype), ve)

    out = lax.map(block, (xb_all, idx, gate))
    return out.reshape(b, s, d)

def setup_inputs(seed: int = 0) -> dict:
    key = jax.random.key(seed)
    ks = jax.random.split(key, 24)
    f32 = jnp.float32
    nrm = lambda k, shape, scale: jax.random.normal(k, shape, f32) * scale
    return {
        "x": nrm(ks[0], (BATCH, SEQ, D_MODEL), 1.0),
        "p": nrm(ks[1], (DEPTH, BATCH, SEQ, PLE_DIM), 1.0),
        "g_mix": 1.0 + nrm(ks[2], (DEPTH, D_MODEL), 0.01),
        "w_in": nrm(ks[3], (DEPTH, D_MODEL, IN_WIDTH), D_MODEL ** -0.5),
        "conv_w": nrm(ks[4], (DEPTH, CONV_K, CONV_WIDTH), CONV_K ** -0.5),
        "conv_b": nrm(ks[5], (DEPTH, CONV_WIDTH), 0.01),
        "w_ret_up": nrm(ks[6], (DEPTH, RET_V, D_MODEL), RET_V ** -0.5),
        "w_conv_up": nrm(ks[7], (DEPTH, CONV_WIDTH, D_MODEL), CONV_WIDTH ** -0.5),
        "w_out": nrm(ks[8], (DEPTH, D_MODEL, D_MODEL), D_MODEL ** -0.5),
        "g_ffn": 1.0 + nrm(ks[9], (DEPTH, D_MODEL), 0.01),
        "w_peer_q": nrm(ks[10], (DEPTH, D_MODEL, PEER_HEADS * PEER_QDIM), D_MODEL ** -0.5),
        "peer_k1": nrm(ks[11], (DEPTH, PEER_HEADS, PEER_NKEYS, PEER_HALF), PEER_HALF ** -0.5),
        "peer_k2": nrm(ks[12], (DEPTH, PEER_HEADS, PEER_NKEYS, PEER_HALF), PEER_HALF ** -0.5),
        "peer_u": nrm(ks[13], (DEPTH, PEER_NEXPERTS, D_MODEL), D_MODEL ** -0.5),
        "peer_v": nrm(ks[14], (DEPTH, PEER_NEXPERTS, D_MODEL), 0.5),
        "g_ple": 1.0 + nrm(ks[15], (DEPTH, D_MODEL), 0.01),
        "w_ple_proj": nrm(ks[16], (DEPTH, PLE_DIM, D_MODEL), PLE_DIM ** -0.5),
        "w_ple_gate": nrm(ks[17], (DEPTH, D_MODEL, D_MODEL), D_MODEL ** -0.5),
        "g_final": 1.0 + nrm(ks[18], (D_MODEL,), 0.01),
    }

def reference(x, p, g_mix, w_in, conv_w, conv_b, w_ret_up, w_conv_up, w_out, g_ffn,
              w_peer_q, peer_k1, peer_k2, peer_u, peer_v, g_ple, w_ple_proj, w_ple_gate, g_final):
    b, s, d = x.shape
    offsets = np.cumsum(IN_SPLITS)[:-1].tolist()
    h = x
    for i in range(DEPTH):
        a = rms_norm(h, g_mix[i])
        proj = a @ w_in[i]
        q, k, v, g_ret, cb, cc, ch, gate_r, gate_c = jnp.split(proj, offsets, axis=-1)
        q = rotary(q.reshape(b, s, RET_HEADS, RET_DK))
        k = rotary(k.reshape(b, s, RET_HEADS, RET_DK)) * (RET_DK ** -0.5)
        v = v.reshape(b, s, RET_HEADS, RET_DV)
        ret = head_group_norm(chunkwise_retention(q, k, v)).reshape(b, s, RET_V)
        ret = (jax.nn.silu(g_ret.astype(jnp.float32)) * ret).astype(x.dtype)
        y_ret = ret @ w_ret_up[i]
        z = causal_short_conv(cc * ch, conv_w[i], conv_b[i])
        y_conv = (cb * z) @ w_conv_up[i]
        merged = jax.nn.sigmoid(gate_r) * y_ret + jax.nn.sigmoid(gate_c) * y_conv
        h = h + merged @ w_out[i]
        h = h + peer_ffn(rms_norm(h, g_ffn[i]), w_peer_q[i], peer_k1[i], peer_k2[i], peer_u[i], peer_v[i])
        ple = p[i] @ w_ple_proj[i]
        h = h + jax.nn.sigmoid(rms_norm(h, g_ple[i]) @ w_ple_gate[i]) * ple
    return rms_norm(h, g_final)


_drawn_inputs = setup_inputs


def setup_inputs(seed=0):
    import zlib

    import numpy as np

    out = dict(_drawn_inputs(seed))
    spreads = {}
    factors = {'conv_b': 3.753, 'g_ffn': 2.716, 'g_ple': 8.0, 'g_final': 5.812}
    for name, (base, spread) in spreads.items():
        noise = np.random.default_rng([zlib.crc32(name.encode()), seed]).standard_normal(out[name].shape)
        drawn = base * np.exp(spread * noise) if base else spread * noise
        out[name] = __import__('jax').numpy.asarray(drawn.astype(out[name].dtype))
    for name, factor in factors.items():
        out[name] = (out[name] * factor).astype(out[name].dtype)
    return out
```

```python
from contextlib import ExitStack

import numpy as np

import concourse.bass as bass
from concourse import mybir

F32 = mybir.dt.float32
F32R = mybir.dt.float32r
BF16 = mybir.dt.bfloat16
U32 = mybir.dt.uint32
ALU = mybir.AluOpType
ACT = mybir.ActivationFunctionType
AX_X = mybir.AxisListType.X

P = 128
D = 1024
T = 1024
DC = D // P
HALF = 512
HEADS, DK, DV = 4, 128, 256
CHUNK = 128
NCH = T // CHUNK
PH, NKEYS, TOPK = 8, 128, 16
TT = T // P
PLE = 256
EPS = 1e-6
LOWEST = -3.0e38
NE = NKEYS

R_PAIR = 0
M1_PAIR = R_PAIR + 3 * HEADS
C_PAIR = M1_PAIR + DC
M2_PAIR = C_PAIR + 3 * DC // 2
O_PAIR = M2_PAIR + DC
Q_PAIR = O_PAIR + DC // 2
A_PAIR = Q_PAIR + PH
P_PAIR = A_PAIR + NE // 2
B_PAIR = P_PAIR + 1
F_PAIR = B_PAIR + NE // 2
PAIRS = F_PAIR + DC // 2
P_MAIN = P_PAIR
F_MAIN = P_MAIN + DC // 2
F_TILE = 2 * B_PAIR

TB = 32
OH = 8
EG = 4

FIRST_HEAD = [("kT", 1), ("scores", 0), ("v0", 0), ("v1", 1), ("kv0", 0), ("kv1", 1)]
HEAD = [("o0", 0), ("o1", 1), ("mean", 0), ("kT", 1), ("scores", 0), ("var", 1), ("v0", 0),
        ("v1", 1), ("kv0", 0), ("kv1", 1)]
LAST = [("o0", 0), ("o1", 1), ("mean", 0), ("var", 1)]


class Scratch:

    def __init__(self, uses, filled, before):
        self.uses, self.filled0, self.before = uses, filled, before

    def at(self, name):
        return [n for n, _ in self.uses].index(name)

    def slot(self, name):
        return self.uses[self.at(name)][1]

    def filled(self, name):
        return self.filled0 + self.at(name) + 1

    def free(self, name):
        s = self.slot(name)
        return self.before[s] + sum(1 for _, x in self.uses[:self.at(name)] if x == s) + 1

    def drained(self, name):
        return self.free(name) + 1


def retention_scratch(h):
    if isinstance(h, int) and h == 0:
        return Scratch(FIRST_HEAD, 1, (1, 0))
    uses = LAST if isinstance(h, int) and h == HEADS else HEAD
    return Scratch(uses, 1 + 6 + 10 * (h - 1), (1 + 3 + 5 * (h - 1), 3 + 5 * (h - 1)))


SCRATCH_R = (1 + 3 + 5 * (HEADS - 1) + 2, 3 + 5 * (HEADS - 1) + 2)
FILLED_R = sum(SCRATCH_R)
NORM1 = Scratch([("stat", 0)], FILLED_R, SCRATCH_R)


def query_scratch(h):
    return Scratch([("s0", 0), ("s1", 1)], FILLED_R + 1 + 2 * h, (SCRATCH_R[0] + 1 + h, SCRATCH_R[1] + h))


FILLED_Q = FILLED_R + 1 + 2 * PH


def select_scratch(tt):
    return Scratch([("sel", 1)], FILLED_Q + tt, (0, SCRATCH_R[1] + PH + tt))


FILLED_A = FILLED_Q + TT
NORM2 = Scratch([("stat", 0)], FILLED_A, (SCRATCH_R[0] + 1 + PH, 0))
NORM3 = Scratch([("stat", 0)], FILLED_A + 1, (SCRATCH_R[0] + 2 + PH, 0))


class Steps:

    def __init__(self, eng, sem):
        self.eng, self.sem, self.n, self.k = eng, sem, 0, 0

    def mark(self, ins):
        ins.then_inc(self.sem, 1)
        self.n, self.k = self.n + 1, self.k + 1

    def then(self, ins):
        self.mark(ins)
        self.eng.wait_ge(self.sem, self.n)

    def enter(self, i, per):
        saved = (self.n, self.k)
        self.n, self.k = self.n + i * per, 0
        return saved, per

    def leave(self, entered, turns):
        (n, k), per = entered
        assert self.k == per, (self.k, per)
        self.n, self.k = n + turns * per, k + turns * per


def build(nc, x_t, p_t, stream, key_t, gains, conv_c, rope, head_c, shape_c, out_t,
          score_d, act_d, gate_d):
    with ExitStack() as ctx:
        def sem(name):
            return ctx.enter_context(nc.semaphore(name))

        def psum(name):
            return ctx.enter_context(nc.psum_tensor(name, [P, 2 * HALF], F32))

        base = (nc.sbuf_base + 31) // 32 * 32
        place = {"at": base}

        def put(name, shape, dt, at=None):
            size = int(np.prod(shape[1:])) * (2 if dt == BF16 else 4)
            size = (size + 31) // 32 * 32
            if at is None:
                at, place["at"] = place["at"], place["at"] + size
            else:
                at, at_next = at[0], at[0] + size
                at_list[0] = at_next
            return nc.alloc_sbuf_tensor_at(name, shape, dt, offset=at)

        at_list = [0]

        def region(start):
            def lay(name, shape, dt):
                t = put(name, shape, dt, at=[at_list[0]])
                return t
            at_list[0] = start
            return lay

        K4 = 4096
        set1 = base
        set2 = set1 + 16 * K4
        res0 = set2 + 16 * K4
        ring0 = res0 + 8 * K4
        tmp0 = ring0 + 6 * K4
        const0 = tmp0 + 5 * K4

        lay = region(const0)
        ident = lay("ident", [P, P], F32)
        iota = lay("iota", [P, P], F32)
        iota16 = lay("iota16", [P, TOPK], F32)
        ones_d = lay("ones_d", [P, P], F32)
        ones_v = lay("ones_v", [P, P], F32)
        gain = lay("gain", [P, 4, DC], F32)
        convc = lay("convc", [P, DC, 4], F32)
        eps_t = lay("eps_t", [P, 1], F32)

        lay = region(ring0)
        raw = lay("raw", [P, 2, D], F32)
        w_hi = lay("w_hi", [P, 2, D], F32R)
        w_lo = lay("w_lo", [P, 2, D], F32R)
        lay = region(set1)
        a_hi = lay("a_hi", [P, DC, T], F32R)
        a_lo = lay("a_lo", [P, DC, T], F32R)
        lay = region(set2)
        mix_hi = lay("mix_hi", [P, DC, T], F32R)
        mix_lo = lay("mix_lo", [P, DC, T], F32R)
        lay = region(res0)
        res = lay("res", [P, DC, T], F32)
        lay = region(tmp0)
        sqb = lay("sqb", [P, 2, T], F32)
        nt0 = lay("nt0", [P, T], F32)
        nt1 = lay("nt1", [P, T], F32)
        nt2 = lay("nt2", [P, T], F32)
        lay = region(tmp0)
        sg = lay("sg", [P, T], F32)
        pbuf = lay("pbuf", [P, T + 2], F32)
        z = lay("z", [P, T], F32)
        lay = region(tmp0)
        p_hi = lay("p_hi", [P, 2, T], F32R)
        p_lo = lay("p_lo", [P, 2, T], F32R)
        p_raw = lay("p_raw", [P, T], F32)
        lay = region(set2)
        cos = lay("cos", [P, T], F32)
        sin = lay("sin", [P, T], F32)
        kT = lay("kT", [P, T], F32)
        qT = lay("qT", [P, T], F32)
        swapped = lay("swapped", [P, T], F32)
        vrow = lay("vrow", [P, T], F32)
        ktok = lay("ktok", [P, NCH, DK], F32)
        vtok = lay("vtok", [P, NCH, DV], F32)
        sdec = lay("sdec", [P, NCH, CHUNK], F32)
        state = lay("state", [P, NCH - 1, DV], F32)
        headc = lay("headc", [P, 2 * CHUNK], F32)
        y = lay("y", [P, 2, T], F32)
        g = lay("g", [P, 2, T], F32)
        headz = nc.alloc_sbuf_tensor_at("headz", [P, 2], F32, offset=const0 + 2560 + 512)
        xi = headc[:, CHUNK:2 * CHUNK]
        lay = region(set1)
        scores = lay("scores", [P, PH * 2, NKEYS], F32)
        gbuf = lay("gbuf", [P, NKEYS, TB], F32)
        actb = lay("actb", [P, 2, T], F32)
        oh2 = lay("oh2", [P, OH, NKEYS], F32R)
        oh1h = lay("oh1h", [P, OH, NKEYS], F32R)
        oh1l = lay("oh1l", [P, OH, NKEYS], F32R)
        eq = lay("eq", [P, PH * TOPK, TOPK], BF16)
        pair_s = lay("pair_s", [P, 2, NKEYS], F32)
        left = lay("left", [P, 2, NKEYS], F32)
        cand = lay("cand", [P, TOPK, TOPK], F32)
        candl = lay("candl", [P, TOPK * TOPK], F32)
        v16 = lay("v16", [P, 2, TOPK], F32)
        ix = lay("ix", [P, 3, TOPK], U32)
        top = lay("top", [P, TOPK], F32)
        sel_ix = lay("sel_ix", [P, PH, 3 * TOPK], U32)
        sel_v = lay("sel_v", [P, PH, TOPK], F32)
        pos_a = lay("pos_a", [P, PH, TOPK], U32)
        pos_b = lay("pos_b", [P, PH, TOPK], U32)
        picked = lay("picked", [P, 3, P], F32)
        gsum = lay("gsum", [P, PH], F32)
        packed = lay("packed", [P, 4, P], F32)
        gate_r = lay("gate_r", [P, P], F32R)
        few = lay("few", [P, 4, TB], F32)
        lay = region(set1 + 2 * K4)
        qrow = lay("qrow", [P, 2, T], F32)
        stage = lay("stage", [P, 2, T], F32)
        keys = lay("keys", [P, 2 * PH, NKEYS], F32)
        lay = region(set1)
        h_hi = lay("h_hi", [P, EG, T], F32R)
        h_lo = lay("h_lo", [P, EG, T], F32R)
        act_in_b = lay("act_in_b", [P, EG, T], F32)
        gate_in = lay("gate_in", [P, T // TB, EG, TB], F32)
        v_hi = lay("v_hi", [P, EG, D], F32R)
        v_lo = lay("v_lo", [P, EG, D], F32R)
        ple = lay("ple", [P, DC, T], F32)
        lay = region(set2)
        fg = lay("fg", [P, 2, T], F32)

        main = [psum("main0"), psum("main1")]
        scr = [psum("scr0"), psum("scr1")]
        bslot = main + scr

        raw_in = [sem("raw_in0"), sem("raw_in1")]
        hi_made = sem("hi_made")
        tile_split = sem("tile_split")
        tile_done = sem("tile_done")
        main_drained = [sem("main_drained0"), sem("main_drained1")]
        scr_filled = sem("scr_filled")
        scr_drained = [sem("scr_drained0"), sem("scr_drained1")]
        consts_in = sem("consts_in")
        rope_in = sem("rope_in")
        x_in = [sem(f"x_in{c}") for c in range(DC)]
        ones_set = sem("ones_set")
        sq_done = sem("sq_done")
        sq_added = sem("sq_added")
        std_done = sem("std_done")
        row_made = sem("row_made")
        row_hi = sem("row_hi")
        row_lo = sem("row_lo")
        dve_step = sem("dve_step")
        headc_in = sem("headc_in")
        kq_ready = sem("kq_ready")
        qxi_ready = sem("qxi_ready")
        states_ready = sem("states_ready")
        ysum_ready = sem("ysum_ready")
        centered = sem("centered")
        ysq_ready = sem("ysq_ready")
        ysqsum_ready = sem("ysqsum_ready")
        gstd_done = sem("gstd_done")
        ret_ready = sem("ret_ready")
        sig_ready = sem("sig_ready")
        merged_done = sem("merged_done")
        z_ready = sem("z_ready")
        z_hi = sem("z_hi")
        z_used = sem("z_used")
        keys_in = sem("keys_in")
        score_st = [sem("score_st0"), sem("score_st1")]
        score_in = sem("score_in")
        head_ranked = sem("head_ranked")
        tops_ready = sem("tops_ready")
        exp_done = sem("exp_done")
        picked_ready = sem("picked_ready")
        onehot_ready = sem("onehot_ready")
        gates_filled = sem("gates_filled")
        gates_drained = sem("gates_drained")
        act_made = sem("act_made")
        act_st = [sem("act_st0"), sem("act_st1")]
        gate_st = sem("gate_st")
        p_in = sem("p_in")
        ple_filled = sem("ple_filled")
        v_hi_made = sem("v_hi_made")
        v_split = sem("v_split")
        act_in = [sem(f"act_in{k}") for k in range(EG)]
        gate_ins = sem("gate_ins")
        h32_ready = sem("h32_ready")
        hhi_ready = sem("hhi_ready")
        h_ready = sem("h_ready")
        b_filled = sem("b_filled")
        b_drained = [sem(f"b_drained{k}") for k in range(4)]
        f_sig = sem("f_sig")
        f_added = sem("f_added")
        out_ready = sem("out_ready")
        out_st = sem("out_st")
        passed = sem("passed")
        passed_pool = sem("passed_pool")

        block = ctx.enter_context(nc.Block())

        @block.sync
        def _(sp):
            def load(pair, s):
                sp.dma_start(raw[:, s, :], stream[bass.ds(2 * pair + s, 1)].rearrange("a p n -> p (a n)")) \
                    .then_inc(raw_in[s], 16)

            sp.dma_start(ident[:, :], shape_c[0]).then_inc(consts_in, 16)
            sp.dma_start(iota[:, :], shape_c[1]).then_inc(consts_in, 16)
            sp.dma_start(iota16[:, :], shape_c[1, :, 0:TOPK]).then_inc(consts_in, 16)
            sp.dma_start(gain[:, :, :], gains).then_inc(consts_in, 16)
            sp.dma_start(convc[:, :, :], conv_c).then_inc(consts_in, 16)
            for c in range(DC):
                sp.dma_start(res[:, c, :], x_t[c * P:(c + 1) * P, :]).then_inc(x_in[c], 16)
                if c == 3:
                    load(0, 0)
                    load(0, 1)
            sp.dma_start(cos[:, :], rope[0]).then_inc(rope_in, 16)
            sp.dma_start(sin[:, :], rope[1]).then_inc(rope_in, 16)
            with sp.Fori(1, B_PAIR) as pair:
                for s in range(2):
                    sp.wait_ge(tile_split, 2 * pair + s - 1)
                    load(pair, s)

            for s in range(2):
                sp.wait_ge(tile_split, 2 * B_PAIR + s - 1)
                load(B_PAIR, s)
            with sp.Fori(1, NE // 2) as i:
                for s in range(2):
                    sp.wait_ge(v_split, 2 * i + s - 1)
                    load(B_PAIR + i, s)
            for s in range(2):
                sp.wait_ge(v_split, NE + s - 1)
                load(F_PAIR, s)
            with sp.Fori(1, DC // 2) as i:
                for s in range(2):
                    sp.wait_ge(tile_split, F_TILE + 2 * i + s - 1)
                    load(F_PAIR + i, s)
            for c in range(DC):
                sp.wait_ge(out_ready, c + 1)
                sp.dma_start(out_t[c * P:(c + 1) * P, :], res[:, c, :]).then_inc(out_st, 16)
            sp.wait_ge(out_st, 16 * DC)

        @block.gpsimd
        def _(pool):
            def split(pair, s, tile, peeled):
                pool.wait_ge(raw_in[s], 16 * pair + 16)
                if not peeled:
                    pool.wait_ge(tile_done, tile - 1)
                pool.sem_inc(passed_pool, 1)
                pool.tensor_copy(w_hi[:, s, :], raw[:, s, :]).then_inc(hi_made, 1)
                pool.wait_ge(hi_made, tile + 1)
                pool.tensor_tensor(w_lo[:, s, :], raw[:, s, :], w_hi[:, s, :].bitcast(F32), ALU.subtract) \
                    .then_inc(tile_split, 1)

            split(0, 0, 0, True)
            split(0, 1, 1, True)
            with pool.Fori(1, B_PAIR) as pair:
                for s in range(2):
                    split(pair, s, 2 * pair + s, False)
            pool.wait_ge(tile_done, 2 * A_PAIR + NE)
            with pool.Fori(0, NE // EG) as b:
                for k in range(EG):
                    s = k % 2
                    pool.wait_ge(raw_in[s], 16 * (B_PAIR + 2 * b + k // 2) + 16)
                    pool.wait_ge(b_filled, 16 * b + 8 * (k // 2) + 8)
                    pool.sem_inc(passed_pool, 1)
                    pool.tensor_copy(v_hi[:, k, :], raw[:, s, :]).then_inc(v_hi_made, 1)
                    pool.wait_ge(v_hi_made, EG * b + k + 1)
                    pool.tensor_tensor(v_lo[:, k, :], raw[:, s, :], v_hi[:, k, :].bitcast(F32), ALU.subtract) \
                        .then_inc(v_split, 1)
            with pool.Fori(0, DC // 2) as i:
                for s in range(2):
                    split(F_PAIR + i, s, F_TILE + 2 * i + s, False)

        @block.tensor
        def _(pe):
            def tile_mm(tile, use, s, rhs_hi, rhs_lo, ready=None):
                pe.wait_ge(tile_split, tile + 1)
                pe.wait_ge(main_drained[s], use + 1)
                for c in range(DC):
                    if ready is not None:
                        pe.wait_ge(row_lo, ready + c + 1)
                    for wt, rows in ((w_hi, rhs_hi), (w_hi, rhs_lo), (w_lo, rhs_hi)):
                        for half in range(2):
                            last = pe.matmul(main[s][:, half * HALF:(half + 1) * HALF],
                                             wt[:, s, c * P:(c + 1) * P],
                                             rows[:, c, half * HALF:(half + 1) * HALF],
                                             start=(c == 0 and wt is w_hi and rows is rhs_hi),
                                             stop=(c == DC - 1 and wt is w_lo))
                last.then_inc(tile_done, 1)

            def fill(m, name):
                pe.wait_ge(scr_drained[m.slot(name)], m.free(name))
                return scr[m.slot(name)]

            def column_mean(m, name, ones, rows):
                slot = fill(m, name)
                for half in range(2):
                    last = pe.matmul(slot[:, half * HALF:(half + 1) * HALF], ones[:, :],
                                     rows[:, half * HALF:(half + 1) * HALF], start=True, stop=True)
                last.then_inc(scr_filled, 1)

            for q in (main_drained[0], main_drained[1], scr_drained[0], scr_drained[1]):
                pe.sem_inc(q, 1)
            for q in b_drained:
                pe.sem_inc(q, 1)
            pe.sem_inc(gates_drained, 2)
            pe.sem_inc(gates_filled, 2)
            pe.sem_inc(b_filled, 16)

            pe.wait_ge(consts_in, 16 * 5)
            pe.wait_ge(ones_set, 3)
            pe.wait_ge(sq_added, DC)
            column_mean(Scratch([("stat", 0)], 0, (0, 0)), "stat", ones_d, nt2)

            def out_part(m, h, e):
                slot = fill(m, f"o{e}")
                for n in range(NCH):
                    dst = slot[:, n * CHUNK:(n + 1) * CHUNK]
                    last = pe.matmul(dst, vtok[:, n, e * P:(e + 1) * P], sdec[:, n, :],
                                     start=True, stop=(n == 0))
                    if n:
                        last = pe.matmul(dst, state[:, n - 1, e * P:(e + 1) * P],
                                         qT[:, n * CHUNK:(n + 1) * CHUNK], start=False, stop=True)
                last.then_inc(scr_filled, 1)

            def to_tokens(m, name, rows):
                slot = fill(m, name)
                for n in range(NCH):
                    last = pe.transpose(slot[:, n * P:(n + 1) * P], rows[:, n * P:(n + 1) * P], ident[:, :])
                last.then_inc(scr_filled, 1)

            def head(h, first=False):
                m = retention_scratch(h)
                tile, use = 6 * h, 3 * h
                tile_mm(tile, use, 0, a_hi, a_lo, ready=0 if first else None)
                if not first:
                    pe.wait_ge(states_ready, h)
                    pe.wait_ge(scr_drained[0], m.free("o0"))
                    out_part(m, h, 0)
                tile_mm(tile + 1, use, 1, a_hi, a_lo)
                if not first:
                    out_part(m, h, 1)
                tile_mm(tile + 2, use + 1, 0, a_hi, a_lo)
                if not first:
                    pe.wait_ge(ysum_ready, h)
                    column_mean(m, "mean", ones_v, nt2)
                pe.wait_ge(kq_ready, 2 * h + 1)
                to_tokens(m, "kT", kT)
                pe.wait_ge(kq_ready, 2 * h + 2)
                slot = fill(m, "scores")
                for n in range(NCH):
                    c = slice(n * CHUNK, (n + 1) * CHUNK)
                    last = pe.matmul(slot[:, c], kT[:, c], qT[:, c], start=True, stop=True)
                last.then_inc(scr_filled, 1)
                tile_mm(tile + 3, use + 1, 1, a_hi, a_lo)
                if not first:
                    pe.wait_ge(ysqsum_ready, h)
                    column_mean(m, "var", ones_v, nt2)
                pe.wait_ge(main_drained[0], use + 3)
                to_tokens(m, "v0", vrow)
                tile_mm(tile + 4, use + 2, 0, a_hi, a_lo)
                pe.wait_ge(main_drained[1], use + 3)
                to_tokens(m, "v1", vrow)
                tile_mm(tile + 5, use + 2, 1, a_hi, a_lo)
                pe.wait_ge(scr_drained[1], m.drained("v1"))
                for e, ns in ((0, range(0, 4)), (1, range(4, NCH - 1))):
                    slot = fill(m, f"kv{e}")
                    for n in ns:
                        last = pe.matmul(slot[:, (n - 4 * e) * DV:(n - 4 * e + 1) * DV], ktok[:, n, :],
                                         vtok[:, n, :], start=True, stop=True)
                    last.then_inc(scr_filled, 1)

            head(0, True)
            with pe.Fori(1, HEADS) as h:
                head(h)
            m = retention_scratch(HEADS)
            pe.wait_ge(states_ready, HEADS)
            out_part(m, HEADS, 0)
            out_part(m, HEADS, 1)
            pe.wait_ge(ysum_ready, HEADS)
            column_mean(m, "mean", ones_v, nt2)
            tile_mm(2 * M1_PAIR, M1_PAIR, 0, a_hi, a_lo)
            pe.wait_ge(ysqsum_ready, HEADS)
            column_mean(m, "var", ones_v, nt2)
            tile_mm(2 * M1_PAIR + 1, M1_PAIR, 1, mix_hi, mix_lo, ready=DC)
            with pe.Fori(1, DC) as n:
                tile_mm(2 * (M1_PAIR + n), M1_PAIR + n, 0, a_hi, a_lo)
                tile_mm(2 * (M1_PAIR + n) + 1, M1_PAIR + n, 1, mix_hi, mix_lo)
            with pe.Fori(0, DC // 2) as i:
                for k in range(6):
                    pair = C_PAIR + 3 * i + k // 2
                    tile_mm(2 * pair + k % 2, pair, k % 2, a_hi, a_lo)
            tile_mm(2 * M2_PAIR, M2_PAIR, 0, a_hi, a_lo)
            pe.wait_ge(z_used, DC + 1)
            tile_mm(2 * M2_PAIR + 1, M2_PAIR, 1, mix_hi, mix_lo)
            with pe.Fori(1, DC) as n:
                tile_mm(2 * (M2_PAIR + n), M2_PAIR + n, 0, a_hi, a_lo)
                tile_mm(2 * (M2_PAIR + n) + 1, M2_PAIR + n, 1, mix_hi, mix_lo)
            with pe.Fori(0, DC // 2) as i:
                for s in range(2):
                    tile_mm(2 * (O_PAIR + i) + s, O_PAIR + i, s, a_hi, a_lo, ready=2 * DC if s == 0 else None)
            pe.wait_ge(sq_added, 2 * DC)
            column_mean(NORM1, "stat", ones_d, nt2)

            def key_scores(h, s):
                m = query_scratch(h)
                pe.wait_ge(main_drained[s], Q_PAIR + h + 2)
                slot = fill(m, f"s{s}")
                for t in range(TT):
                    last = pe.matmul(slot[:, t * P:(t + 1) * P], qrow[:, s, t * P:(t + 1) * P],
                                     keys[:, bass.ds(2 * h + s, 1), :].rearrange("p a n -> p (a n)"),
                                     start=True, stop=True)
                last.then_inc(scr_filled, 1)

            def queries(h, first=False):
                tile_mm(2 * (Q_PAIR + h), Q_PAIR + h, 0, mix_hi, mix_lo, ready=3 * DC if first else None)
                if not first:
                    key_scores(h - 1, 1)
                tile_mm(2 * (Q_PAIR + h) + 1, Q_PAIR + h, 1, mix_hi, mix_lo)
                key_scores(h, 0)

            pe.wait_ge(keys_in, 16)
            queries(0, True)
            with pe.Fori(1, PH) as h:
                queries(h)
            key_scores(PH - 1, 1)

            def gates(block4, w):
                pe.wait_ge(onehot_ready, block4 + 2)
                pe.wait_ge(gates_drained, block4 + 1)
                for k in range(4):
                    dst = scr[0][:, w * HALF + k * P:w * HALF + (k + 1) * P]
                    pe.matmul(dst, oh2[:, 4 * w + k, :], oh1h[:, 4 * w + k, :], start=True, stop=False)
                    last = pe.matmul(dst, oh2[:, 4 * w + k, :], oh1l[:, 4 * w + k, :], start=False, stop=True)
                last.then_inc(gates_filled, 1)

            def expert_tiles(tt, i, first):
                def quarter(q):
                    for w in range(2):
                        gates(32 * tt + 8 * i + 2 * q + w, w)

                for q in range(4):
                    pair = A_PAIR + 8 * tt + 2 * i + q // 2
                    tile_mm(2 * pair + q % 2, pair, q % 2, mix_hi, mix_lo)
                    if first and q == 0:
                        m = select_scratch(tt)
                        pe.wait_ge(picked_ready, tt + 1)
                        slot = fill(m, "sel")
                        for k in range(3):
                            last = pe.transpose(slot[:, k * P:(k + 1) * P], picked[:, k, :], ident[:, :])
                        last.then_inc(scr_filled, 1)
                    elif first:
                        quarter(q - 1)
                    else:
                        quarter(q)
                if first:
                    quarter(3)

            pe.wait_ge(scr_drained[0], query_scratch(PH - 1).drained("s0"))
            with pe.Fori(0, TT) as tt:
                expert_tiles(tt, 0, True)
                with pe.Fori(1, 4) as i:
                    expert_tiles(tt, i, False)

            for n in range(DC):
                s = n % 2
                if n % 4 == 0:
                    pe.wait_ge(tile_split, 2 * P_PAIR + n // 4 + 1)
                    pe.wait_ge(row_lo, 4 * DC + 2)
                pe.wait_ge(main_drained[s], P_MAIN + n // 2 + 1)
                for c in range(2):
                    col = (n % 4 * 2 + c) * P
                    for wt, rows in ((w_hi, p_hi), (w_hi, p_lo), (w_lo, p_hi)):
                        for half in range(2):
                            last = pe.matmul(main[s][:, half * HALF:(half + 1) * HALF],
                                             wt[:, n // 4, col:col + P], rows[:, c, half * HALF:(half + 1) * HALF],
                                             start=(c == 0 and wt is w_hi and rows is p_hi),
                                             stop=(c == 1 and wt is w_lo))
                last.then_inc(tile_done if n % 4 == 3 else ple_filled, 1)

            def pairs_of_experts(b):
                for e in range(2):
                    pe.wait_ge(v_split, EG * b + 2 * e + 2)
                    pe.wait_ge(h_ready, EG * b + 2 * e + 2)
                    for dt in range(DC):
                        slot = bslot[dt % 4]
                        pe.wait_ge(b_drained[dt % 4], 4 * b + 2 * e + dt // 4 + 1)
                        for k in (2 * e, 2 * e + 1):
                            for vt, ht in ((v_hi, h_hi), (v_hi, h_lo), (v_lo, h_hi)):
                                for half in range(2):
                                    last = pe.matmul(slot[:, half * HALF:(half + 1) * HALF],
                                                     vt[:, k, dt * P:(dt + 1) * P],
                                                     ht[:, k, half * HALF:(half + 1) * HALF],
                                                     start=(k % 2 == 0 and vt is v_hi and ht is h_hi),
                                                     stop=(k % 2 == 1 and vt is v_lo))
                        last.then_inc(b_filled, 1)

            for s in range(2):
                pe.wait_ge(main_drained[s], F_MAIN + 1)
            pe.wait_ge(gates_drained, 2 + T // 4)
            pe.wait_ge(scr_drained[1], select_scratch(TT - 1).drained("sel"))
            with pe.Fori(0, NE // EG) as b:
                pairs_of_experts(b)

            pe.wait_ge(sq_added, 3 * DC)
            column_mean(NORM2, "stat", ones_d, nt2)
            with pe.Fori(0, DC // 2) as i:
                for s in range(2):
                    tile_mm(F_TILE + 2 * i + s, F_MAIN + i, s, a_hi, a_lo, ready=4 * DC + 2 if s == 0 else None)
            pe.wait_ge(sq_added, 4 * DC)
            column_mean(NORM3, "stat", ones_d, nt2)

        @block.scalar
        def _(act):
            def square(i, src, peeled=False):
                if not peeled:
                    act.wait_ge(sq_added, i - 1)
                act.activation(sqb[:, i % 2, :] if isinstance(i, int) else None, src, ACT.Square) \
                    .then_inc(sq_done, 1)

            def rough_rstd(slot, done, count):
                act.activation(nt0[:, :], slot[:, :], ACT.Ln, bias=eps_t[:, 0:1]).then_inc(done, 1)
                act.wait_ge(done, count + 1)
                act.activation(nt0[:, :], nt0[:, :], ACT.Exp, scale=-0.5).then_inc(done, 1)

            def norm_std(m, count):
                act.wait_ge(scr_filled, m.filled("stat"))
                rough_rstd(scr[0], std_done, 2 * count)

            def hi_rows(dst, first, n, src=None, made=None):
                for c in range(n):
                    act.wait_ge(row_made, first + c + 1)
                    act.copy(dst[:, c, :], sqb[:, c % 2, :] if src is None else src(c)).then_inc(row_hi, 1)

            act.sem_inc(act_st[0], 16)
            act.sem_inc(act_st[1], 16)
            act.sem_inc(gate_st, 16)
            act.sem_inc(score_st[0], 16)
            act.sem_inc(score_st[1], 16)

            act.dma_start(headc[:, :], head_c[0, :, 0:2 * CHUNK]).then_inc(headc_in, 16)
            act.dma_start(headz[:, :], head_c[0, :, 2 * CHUNK:2 * CHUNK + 2]).then_inc(headc_in, 16)
            act.wait_ge(ones_set, 3)
            for c in range(DC):
                act.wait_ge(x_in[c], 16)
                square(c, res[:, c, :], peeled=c < 2)
            norm_std(Scratch([("stat", 0)], 0, (0, 0)), 0)
            hi_rows(a_hi, 0, DC)

            def head(h, first=False, last=False):
                m = retention_scratch(h)
                if not first:
                    for e in range(2):
                        act.wait_ge(scr_filled, m.filled(f"o{e}"))
                        act.wait_ge(ret_ready, 2 * h - 1)
                        act.copy(y[:, e, :], scr[e][:, :]).then_inc(scr_drained[e], 1)
                if not last:
                    if not first:
                        act.wait_ge(states_ready, h)
                        hc = head_c[bass.ds(h, 1)].rearrange("a p n -> p (a n)")
                        act.dma_start(headc[:, :], hc[:, 0:2 * CHUNK]).then_inc(headc_in, 16)
                        act.dma_start(headz[:, :], hc[:, 2 * CHUNK:2 * CHUNK + 2]).then_inc(headc_in, 16)
                    act.wait_ge(tile_done, 6 * h + 3)
                    act.copy(vrow[:, :], main[0][:, :]).then_inc(main_drained[0], 1)
                if not first:
                    for e in range(2):
                        act.wait_ge(centered, 2 * h - 1 + e)
                        act.activation(sqb[:, e, :], y[:, e, :], ACT.Square).then_inc(ysq_ready, 1)
                if not last:
                    act.wait_ge(scr_filled, m.filled("kT"))
                    act.wait_ge(headc_in, 32 * h + 32)
                    act.activation(ktok[:, :, :].rearrange("p n k -> p (n k)"), scr[1][:, :], ACT.Copy,
                                   scale=headz[:, 0:1]).then_inc(scr_drained[1], 1)
                if not first:
                    act.wait_ge(scr_filled, m.filled("var"))
                    rough_rstd(scr[1], gstd_done, 2 * (h - 1))
                if not last:
                    act.wait_ge(scr_filled, m.filled("v0"))
                    act.copy(vtok[:, :, 0:P], scr[0][:, :].rearrange("p (n k) -> p n k", n=NCH)) \
                        .then_inc(scr_drained[0], 1)
                    act.wait_ge(tile_done, 6 * h + 4)
                    act.copy(vrow[:, :], main[1][:, :]).then_inc(main_drained[1], 1)
                    act.wait_ge(tile_done, 6 * h + 5)
                    if not first:
                        act.wait_ge(ret_ready, 2 * h + 1)
                    act.activation(g[:, 0, :], main[0][:, :], ACT.Sigmoid).then_inc(sig_ready, 1)
                    act.wait_ge(scr_filled, m.filled("v1"))
                    act.copy(vtok[:, :, P:DV], scr[1][:, :].rearrange("p (n k) -> p n k", n=NCH)) \
                        .then_inc(scr_drained[1], 1)
                    act.wait_ge(tile_done, 6 * h + 6)
                    act.activation(g[:, 1, :], main[1][:, :], ACT.Sigmoid).then_inc(sig_ready, 1)

            head(0, first=True)
            with act.Fori(1, HEADS) as h:
                head(h)
            head(HEADS, last=True)
            act.wait_ge(ret_ready, 2 * HEADS + 1)
            hi_rows(mix_hi, DC, DC, src=lambda c: res[:, c, :])

            with act.Fori(0, DC) as n:
                act.wait_ge(tile_done, 2 * (M1_PAIR + n) + 1)
                act.wait_ge(merged_done, n + 1)
                act.activation(sg[:, :], main[0][:, :], ACT.Sigmoid).then_inc(main_drained[0], 1)
            with act.Fori(0, DC // 2) as i:
                for k in range(2):
                    pair = C_PAIR + 3 * i + (3 * k) // 2
                    s = k
                    act.wait_ge(tile_done, 2 * pair + s + 1)
                    act.wait_ge(merged_done, DC + 2 * i + k + 1)
                    act.copy(sg[:, :], main[s][:, :]).then_inc(main_drained[s], 1)
                    act.wait_ge(z_ready, 2 * i + k + 1)
                    act.copy(mix_hi[:, bass.ds(2 * i + k, 1), :].rearrange("p a t -> p (a t)"), z[:, :]) \
                        .then_inc(z_hi, 1)
            with act.Fori(0, DC) as n:
                act.wait_ge(tile_done, 2 * (M2_PAIR + n) + 1)
                act.wait_ge(merged_done, 2 * DC + n + 1)
                act.activation(sg[:, :], main[0][:, :], ACT.Sigmoid).then_inc(main_drained[0], 1)
            hi_rows(a_hi, 2 * DC, DC, src=lambda c: res[:, c, :])
            for c in range(DC):
                act.wait_ge(row_lo, 2 * DC + c + 1)
                act.dma_start(res[:, c, :], x_t[c * P:(c + 1) * P, :]).then_inc(x_in[c], 16)
            with act.Fori(0, DC // 2) as i:
                for s in range(2):
                    act.wait_ge(main_drained[s], O_PAIR + i + 2)
                    act.wait_ge(sq_added, DC + 2 * i + s - 1)
                    act.activation(sqb[:, s, :], res[:, bass.ds(2 * i + s, 1), :].rearrange("p a t -> p (a t)"),
                                   ACT.Square).then_inc(sq_done, 1)
            norm_std(NORM1, 1)
            act.dma_start(keys[:, :, :], key_t).then_inc(keys_in, 16)
            hi_rows(mix_hi, 3 * DC, DC)

            def query(h, s):
                act.wait_ge(tile_done, 2 * (Q_PAIR + h) + s + 1)
                act.copy(qrow[:, s, :], main[s][:, :]).then_inc(main_drained[s], 1)

            def scores_out(h, s):
                m = query_scratch(h)
                act.wait_ge(scr_filled, m.filled(f"s{s}"))
                act.wait_ge(score_st[s], 16 * h + 16)
                act.wait_ge(head_ranked, h + 1)
                act.copy(stage[:, s, :], scr[s][:, :]).then_inc(scr_drained[s], 1)
                act.wait_ge(scr_drained[s], m.drained(f"s{s}"))
                act.dma_start(score_d[:, :, bass.ds(2 * h + s, 1), :].rearrange("t p a n -> p t (a n)"),
                              stage[:, s, :].rearrange("p (t n) -> p t n", t=TT)).then_inc(score_st[s], 16)

            query(0, 0)
            query(0, 1)
            scores_out(0, 0)
            with act.Fori(1, PH) as h:
                query(h, 0)
                scores_out(h - 1, 1)
                query(h, 1)
                scores_out(h, 0)
            scores_out(PH - 1, 1)

            def softmax(tt):
                act.wait_ge(tops_ready, tt + 1)
                act.activation(sel_v[:, :, :], sel_v[:, :, :], ACT.Exp).then_inc(exp_done, 1)

            for c in range(2):
                if c:
                    act.wait_ge(row_lo, 4 * DC + 1)
                act.dma_start(p_raw[:, :], p_t[c * P:(c + 1) * P, :]).then_inc(p_in, 16)
                act.wait_ge(p_in, 16 * c + 16)
                act.copy(p_hi[:, c, :], p_raw[:, :]).then_inc(row_hi, 1)

            softmax(0)
            for s in range(2):
                act.wait_ge(score_st[s], 16 * PH + 16)

            def expert_tiles(tt, i, first, last):
                def quarter(q):
                    for w in range(2):
                        block4 = 32 * tt + 8 * i + 2 * q + w
                        act.wait_ge(gates_filled, block4 + 3)
                        if q == 0 and w == 0:
                            act.wait_ge(gate_st, 16 * (4 * tt + i) + 16)
                        act.copy(gbuf[:, :, 8 * q + 4 * w:8 * q + 4 * w + 4].rearrange("p e t -> p t e"),
                                 scr[0][:, w * HALF:(w + 1) * HALF].rearrange("p (t e) -> p t e", t=4)) \
                            .then_inc(gates_drained, 1)

                if first and not last:
                    act.wait_ge(head_ranked, PH * (tt + 1) + 1)
                    act.dma_start(scores[:, :, :], score_d[bass.ds(tt + 1, 1)].rearrange("a p h n -> p (a h) n")) \
                        .then_inc(score_in, 16)
                for q in range(4):
                    pair = A_PAIR + 8 * tt + 2 * i + q // 2
                    e = 16 * tt + 4 * i + q
                    s = q % 2
                    act.wait_ge(tile_done, 2 * pair + s + 1)
                    act.wait_ge(act_st[s], 16 * (8 * tt + 2 * i + q // 2) + 16)
                    act.activation(actb[:, s, :], main[s][:, :], ACT.Gelu).then_inc(main_drained[s], 1)
                    if first and q:
                        quarter(q - 1)
                    elif not first:
                        quarter(q)
                    act.wait_ge(main_drained[s], pair + 2)
                    act.dma_start(act_d[bass.ds(e, 1)].rearrange("a p n -> p (a n)"), actb[:, s, :]) \
                        .then_inc(act_st[s], 16)
                if first:
                    quarter(3)
                act.wait_ge(gates_drained, 2 + 32 * tt + 8 * i + 8)
                act.dma_start(gate_d[bass.ds(4 * tt + i, 1)].rearrange("a p e t -> p (a e t)"),
                              gbuf[:, :, :].rearrange("p e t -> p (e t)")).then_inc(gate_st, 16)

            with act.Fori(0, TT - 1) as tt:
                expert_tiles(tt, 0, True, False)
                with act.Fori(1, 4) as i:
                    expert_tiles(tt, i, False, False)
                softmax(tt + 1)
            expert_tiles(TT - 1, 0, True, True)
            with act.Fori(1, 4) as i:
                expert_tiles(TT - 1, i, False, True)

            def ple_out(ns):
                for n in ns:
                    s = n % 2
                    if n % 4 == 3:
                        act.wait_ge(tile_done, 2 * P_PAIR + n // 4 + 1)
                    else:
                        act.wait_ge(ple_filled, n - n // 4 + 1)
                    act.copy(ple[:, n, :], main[s][:, :]).then_inc(main_drained[s], 1)

            def load_act(b, k):
                act.dma_start(act_in_b[:, k, :], act_d[bass.ds(EG * b + k, 1)].rearrange("a p n -> p (a n)")) \
                    .then_inc(act_in[k], 16)

            def load_gates(b, blocks=slice(0, T // TB)):
                act.dma_start(gate_in[:, blocks, :, :].rearrange("p b e t -> p b (e t)"),
                              gate_d[blocks, :, bass.ds(EG * b, EG), :].rearrange("b p e t -> p b (e t)")) \
                    .then_inc(gate_ins, 16)

            act.wait_ge(gates_filled, 2 + T // 4)
            for q in act_st:
                act.wait_ge(q, 16 + 16 * (NE // 2))
            for k in range(EG):
                load_act(0, k)
            act.wait_ge(gate_st, 16 + 16 * (T // TB - 1))
            load_gates(0, slice(0, T // TB - 1))
            ple_out(range(0, 4))
            act.wait_ge(gate_st, 16 + 16 * (T // TB))
            load_gates(0, slice(T // TB - 1, T // TB))
            ple_out(range(4, DC))

            def hi_of_round(b, last=False):
                for k in range(EG):
                    act.wait_ge(h32_ready, EG * b + k + 1)
                    act.wait_ge(b_filled, 16 * b + 8 * (k // 2) + 8)
                    act.copy(h_hi[:, k, :], act_in_b[:, k, :]).then_inc(hhi_ready, 1)
                    if last:
                        continue
                    if k == 0:
                        act.wait_ge(h32_ready, EG * b + EG)
                        load_gates(b + 1)
                    elif k % 2:
                        for q in (k - 1, k):
                            act.wait_ge(h_ready, EG * b + q + 1)
                            load_act(b + 1, q)

            with act.Fori(0, NE // EG - 1) as b:
                hi_of_round(b)
            hi_of_round(NE // EG - 1, last=True)

            for c in range(DC):
                act.wait_ge(b_drained[c % 4], 4 * (NE // EG) + 1)
                square(2 * DC + c, res[:, c, :])
            norm_std(NORM2, 2)
            hi_rows(a_hi, 4 * DC, DC)
            with act.Fori(0, DC // 2) as i:
                for s in range(2):
                    act.wait_ge(tile_done, F_TILE + 2 * i + s + 1)
                    act.wait_ge(f_added, 2 * i + s + 1)
                    act.activation(fg[:, s, :], main[s][:, :], ACT.Sigmoid).then_inc(main_drained[s], 1)
                    act.wait_ge(f_added, 2 * i + s + 3)
                    act.wait_ge(sq_added, 3 * DC + 2 * i + s - 1)
                    act.activation(sqb[:, s, :], res[:, bass.ds(2 * i + s, 1), :].rearrange("p a t -> p (a t)"),
                                   ACT.Square).then_inc(sq_done, 1)
            norm_std(NORM3, 3)

        @block.vector
        def _(dve):
            steps = Steps(dve, dve_step)

            def add_square(i, first, s):
                dve.wait_ge(sq_done, i + 1)
                if first:
                    dve.tensor_copy(nt2[:, :], sqb[:, s, :]).then_inc(sq_added, 1)
                else:
                    dve.wait_ge(sq_added, i)
                    dve.tensor_tensor(nt2[:, :], nt2[:, :], sqb[:, s, :], ALU.add).then_inc(sq_added, 1)

            def newton(slot, drained):
                dve.tensor_scalar(nt1[:, :], slot[:, :], -0.5, -0.5 * EPS, ALU.mult, ALU.add).then_inc(drained, 1)
                steps.then(dve.tensor_tensor(nt2[:, :], nt0[:, :], nt0[:, :], ALU.mult))

            def newton_end(drained, value):
                dve.wait_ge(drained, value)
                steps.then(dve.tensor_tensor(nt2[:, :], nt2[:, :], nt1[:, :], ALU.mult))
                steps.then(dve.scalar_tensor_tensor(nt0[:, :], nt2[:, :], 1.5, nt0[:, :], ALU.add, ALU.mult))

            def norm_rstd(m, count):
                dve.wait_ge(std_done, 2 * count + 2)
                newton(scr[0], scr_drained[0])
                newton_end(scr_drained[0], m.drained("stat"))

            def norm_rows(first, which, dst_lo, dst_hi):
                def row(c):
                    if c >= 2:
                        dve.wait_ge(row_lo, first + c - 1)
                    dve.scalar_tensor_tensor(sqb[:, c % 2, :], res[:, c, :], gain[:, which, c:c + 1], nt0[:, :],
                                             ALU.mult, ALU.mult).then_inc(row_made, 1)
                row(0)
                for c in range(DC):
                    if c + 1 < DC:
                        row(c + 1)
                    dve.wait_ge(row_hi, first + c + 1)
                    dve.tensor_tensor(dst_lo[:, c, :], sqb[:, c % 2, :], dst_hi[:, c, :].bitcast(F32),
                                      ALU.subtract).then_inc(row_lo, 1)

            dve.memset(ones_d[:, :], 1.0 / D).then_inc(ones_set, 1)
            dve.memset(ones_v[:, :], 1.0 / DV).then_inc(ones_set, 1)
            dve.memset(eps_t[:, :], EPS).then_inc(ones_set, 1)
            dve.sem_inc(ret_ready, 1)
            dve.sem_inc(merged_done, 1)
            dve.sem_inc(z_used, 1)
            dve.sem_inc(onehot_ready, 1)
            dve.sem_inc(head_ranked, 1)
            dve.sem_inc(f_added, 2)
            dve.wait_ge(consts_in, 16 * 5)
            for c in range(DC):
                add_square(c, c == 0, c % 2)
            norm_rstd(Scratch([("stat", 0)], 0, (0, 0)), 0)
            norm_rows(0, 0, a_lo, a_hi)
            dve.wait_ge(rope_in, 32)

            def rotary(dst, s):
                steps.mark(dve.tensor_tensor(dst[:, :], main[s][:, :], cos[:, :], ALU.mult))
                steps.mark(dve.tensor_copy(swapped[0:64, :], main[s][64:128, :]))
                dve.tensor_copy(swapped[64:128, :], main[s][0:64, :]).then_inc(main_drained[s], 1)

            def rotary_end(dst):
                steps.then(dve.tensor_tensor(swapped[:, :], swapped[:, :], sin[:, :], ALU.mult))
                dve.tensor_tensor(dst[:, :], dst[:, :], swapped[:, :], ALU.add).then_inc(kq_ready, 1)

            def head(h, first=False, last=False):
                m = retention_scratch(h)
                if not last:
                    for s, dst in ((0, kT), (1, qT)):
                        dve.wait_ge(tile_done, 6 * h + s + 1)
                        if s and not first:
                            dve.wait_ge(scr_filled, m.filled("o1"))
                        if not (first and s == 0):
                            dve.wait_ge(kq_ready, 2 * h + s)
                        rotary(dst, s)
                        dve.wait_ge(dve_step, steps.n)
                        dve.wait_ge(main_drained[s], 3 * h + 2)
                        rotary_end(dst)
                if not first:
                    for e in range(2):
                        dve.wait_ge(scr_drained[e], m.drained(f"o{e}"))
                    dve.tensor_tensor(nt2[:, :], y[:, 0, :], y[:, 1, :], ALU.add).then_inc(ysum_ready, 1)
                    dve.wait_ge(scr_filled, m.filled("mean"))
                    for e in range(2):
                        dve.tensor_tensor(y[:, e, :], y[:, e, :], scr[0][:, :], ALU.subtract).then_inc(centered, 1)
                    dve.wait_ge(centered, 2 * h)
                    dve.sem_inc(scr_drained[0], 1)
                if not last:
                    dve.wait_ge(scr_filled, m.filled("scores"))
                    dve.wait_ge(headc_in, 32 * h + 32)
                    dve.tensor_tensor(sdec[:, :, :], scr[0][:, :].rearrange("p (n i) -> p n i", n=NCH),
                                      headc[:, 0:CHUNK].unsqueeze(1).to_broadcast([P, NCH, CHUNK]),
                                      ALU.mult).then_inc(scr_drained[0], 1)
                    q3 = qT[:, :].rearrange("p (n i) -> p n i", n=NCH)
                    dve.wait_ge(kq_ready, 2 * h + 2)
                    dve.tensor_tensor(q3, q3, xi.unsqueeze(1).to_broadcast([P, NCH, CHUNK]), ALU.mult) \
                        .then_inc(qxi_ready, 1)
                if not first:
                    dve.wait_ge(ysq_ready, 2 * h)
                    dve.tensor_tensor(nt2[:, :], sqb[:, 0, :], sqb[:, 1, :], ALU.add).then_inc(ysqsum_ready, 1)
                    dve.wait_ge(gstd_done, 2 * h)
                    newton(scr[1], scr_drained[1])
                    newton_end(scr_drained[1], m.drained("var"))
                    for e in range(2):
                        steps.mark(dve.tensor_tensor(y[:, e, :], y[:, e, :], nt0[:, :], ALU.mult))
                    dve.wait_ge(dve_step, steps.n)
                    for e in range(2):
                        dve.tensor_tensor(res[:, bass.ds(2 * (h - 1) + e, 1), :].rearrange("p a t -> p (a t)")
                                          if not isinstance(h, int) else res[:, 2 * (h - 1) + e, :],
                                          y[:, e, :], g[:, e, :], ALU.mult).then_inc(ret_ready, 1)
                if not last:
                    for e in range(2):
                        dve.wait_ge(sig_ready, 2 * h + e + 1)
                        dve.tensor_tensor(g[:, e, :], g[:, e, :], main[e][:, :], ALU.mult) \
                            .then_inc(main_drained[e], 1)
                    for e, ns in ((0, range(0, 4)), (1, range(4, NCH - 1))):
                        dve.wait_ge(scr_filled, m.filled(f"kv{e}"))
                        for n in ns:
                            kv = scr[e][:, (n - 4 * e) * DV:(n - 4 * e + 1) * DV]
                            if n == 0:
                                ins = dve.tensor_copy(state[:, 0, :], kv)
                            else:
                                ins = dve.scalar_tensor_tensor(state[:, n, :], state[:, n - 1, :], headz[:, 1:2],
                                                               kv, ALU.mult, ALU.add)
                            if n == 3:
                                ins.then_inc(scr_drained[0], 1)
                                dve.wait_ge(scr_drained[0], m.drained("kv0"))
                            elif n == NCH - 2:
                                ins.then_inc(scr_drained[1], 1)
                                dve.wait_ge(scr_drained[1], m.drained("kv1"))
                                dve.sem_inc(states_ready, 1)
                            else:
                                steps.then(ins)

            head(0, first=True)
            with dve.Fori(1, HEADS) as h:
                inside = steps.enter(h - 1, 6 + 3 + 2 + 5)
                head(h)
                steps.leave(inside, HEADS - 1)
            head(HEADS, last=True)

            def lo_of(first, dst_lo, dst_hi, src):
                for c in range(DC):
                    dve.wait_ge(row_hi, first + c + 1)
                    dve.tensor_tensor(dst_lo[:, c, :], src[:, c, :], dst_hi[:, c, :].bitcast(F32), ALU.subtract) \
                        .then_inc(row_lo, 1)

            dve.wait_ge(ret_ready, 2 * HEADS + 1)
            dve.sem_inc(row_made, DC)
            lo_of(DC, mix_lo, mix_hi, res)
            with dve.Fori(0, DC) as n:
                dve.wait_ge(main_drained[0], M1_PAIR + n + 2)
                dve.wait_ge(tile_done, 2 * (M1_PAIR + n) + 2)
                dve.tensor_tensor(res[:, bass.ds(n, 1), :].rearrange("p a t -> p (a t)"), main[1][:, :], sg[:, :],
                                  ALU.mult).then_inc(main_drained[1], 1)
                dve.wait_ge(main_drained[1], M1_PAIR + n + 2)
                dve.sem_inc(merged_done, 1)

            dve.memset(pbuf[:, 0:2], 0.0).then_inc(ones_set, 1)
            dve.wait_ge(ones_set, 4)
            with dve.Fori(0, DC // 2) as i:
                inside = steps.enter(i, 2 * 3)
                for k in range(2):
                    tiles = [3 * k, 3 * k + 1, 3 * k + 2]
                    s_ch, s_cb = tiles[1] % 2, tiles[2] % 2
                    pair_ch, pair_cb = C_PAIR + 3 * i + tiles[1] // 2, C_PAIR + 3 * i + tiles[2] // 2
                    j = 2 * i + k

                    def c_of(q):
                        return convc[:, bass.ds(j, 1), q:q + 1].rearrange("p a q -> p (a q)")

                    dve.wait_ge(main_drained[k], C_PAIR + 3 * i + tiles[0] // 2 + 2)
                    dve.wait_ge(tile_done, 2 * pair_ch + s_ch + 1)
                    dve.tensor_tensor(pbuf[:, 2:T + 2], main[s_ch][:, :], sg[:, :], ALU.mult) \
                        .then_inc(main_drained[s_ch], 1)
                    dve.wait_ge(main_drained[s_ch], pair_ch + 2)
                    dve.sem_inc(merged_done, 1)
                    dve.wait_ge(z_used, j + 1)
                    steps.then(dve.tensor_scalar(z[:, :], pbuf[:, 2:T + 2], c_of(2), c_of(3), ALU.mult, ALU.add))
                    steps.then(dve.scalar_tensor_tensor(z[:, :], pbuf[:, 1:T + 1], c_of(1), z[:, :],
                                                        ALU.mult, ALU.add))
                    steps.then(dve.scalar_tensor_tensor(z[:, :], pbuf[:, 0:T], c_of(0), z[:, :],
                                                        ALU.mult, ALU.add))
                    dve.wait_ge(tile_done, 2 * pair_cb + s_cb + 1)
                    dve.tensor_tensor(z[:, :], main[s_cb][:, :], z[:, :], ALU.mult).then_inc(main_drained[s_cb], 1)
                    dve.wait_ge(main_drained[s_cb], pair_cb + 2)
                    dve.sem_inc(z_ready, 1)
                    dve.wait_ge(z_hi, j + 1)
                    dve.tensor_tensor(mix_lo[:, bass.ds(j, 1), :].rearrange("p a t -> p (a t)"), z[:, :],
                                      mix_hi[:, bass.ds(j, 1), :].rearrange("p a t -> p (a t)").bitcast(F32),
                                      ALU.subtract).then_inc(z_used, 1)
                steps.leave(inside, DC // 2)
            with dve.Fori(0, DC) as n:
                inside = steps.enter(n, 1)
                r = res[:, bass.ds(n, 1), :].rearrange("p a t -> p (a t)")
                dve.wait_ge(main_drained[0], M2_PAIR + n + 2)
                dve.wait_ge(tile_done, 2 * (M2_PAIR + n) + 2)
                dve.tensor_tensor(sg[:, :], main[1][:, :], sg[:, :], ALU.mult).then_inc(main_drained[1], 1)
                dve.wait_ge(main_drained[1], M2_PAIR + n + 2)
                steps.then(dve.tensor_tensor(r, r, sg[:, :], ALU.add))
                dve.sem_inc(merged_done, 1)
                steps.leave(inside, DC)
            steps.then(dve.memset(nt2[:, :], 0.0))
            dve.sem_inc(row_made, DC)
            lo_of(2 * DC, a_lo, a_hi, res)
            for c in range(DC):
                dve.wait_ge(x_in[c], 32)
            with dve.Fori(0, DC // 2) as i:
                for s in range(2):
                    r = res[:, bass.ds(2 * i + s, 1), :].rearrange("p a t -> p (a t)")
                    dve.wait_ge(tile_done, 2 * (O_PAIR + i) + s + 1)
                    dve.tensor_tensor(r, main[s][:, :], r, ALU.add).then_inc(main_drained[s], 1)
                    if s == 0:
                        dve.wait_ge(sq_done, DC + 2 * i + 1)
                        dve.wait_ge(sq_added, DC + 2 * i)
                    else:
                        dve.wait_ge(sq_done, DC + 2 * i + 2)
                        dve.wait_ge(sq_added, DC + 2 * i + 1)
                    dve.tensor_tensor(nt2[:, :], nt2[:, :], sqb[:, s, :], ALU.add).then_inc(sq_added, 1)
            norm_rstd(NORM1, 1)
            norm_rows(3 * DC, 1, mix_lo, mix_hi)

            def settled():
                dve.wait_ge(dve_step, steps.n)
                dve.sem_inc(passed, 1)

            def rank(s1, s2, h):
                src = (s1, s2)
                settled()
                for s in range(2):
                    steps.mark(dve.max(v16[:, s, 0:8], src[s]))
                settled()
                for s in range(2):
                    steps.mark(dve.max_index(ix[:, s, 0:8], v16[:, s, 0:8], src[s]))
                    steps.mark(dve.match_replace(left[:, s, :], v16[:, s, 0:8], src[s], LOWEST))
                settled()
                for s in range(2):
                    steps.mark(dve.max(v16[:, s, 8:16], left[:, s, :]))
                settled()
                for s in range(2):
                    steps.mark(dve.max_index(ix[:, s, 8:16], v16[:, s, 8:16], left[:, s, :]))
                settled()
                steps.mark(dve.tensor_tensor(cand[:, :, :], v16[:, 0, :].unsqueeze(2).to_broadcast([P, TOPK, TOPK]),
                                             v16[:, 1, :].unsqueeze(1).to_broadcast([P, TOPK, TOPK]), ALU.add))
                flat = cand[:, :, :].rearrange("p a b -> p (a b)")
                settled()
                steps.mark(dve.max(top[:, 0:8], flat))
                settled()
                steps.mark(dve.max_index(ix[:, 2, 0:8], top[:, 0:8], flat))
                steps.mark(dve.match_replace(candl[:, :], top[:, 0:8], flat, LOWEST))
                settled()
                steps.mark(dve.max(top[:, 8:16], candl[:, :]))
                settled()
                steps.mark(dve.max_index(ix[:, 2, 8:16], top[:, 8:16], candl[:, :]))
                settled()
                steps.mark(dve.tensor_copy(sel_ix[:, bass.ds(h, 1), :].rearrange("p a k -> p (a k)"),
                                           ix[:, :, :].rearrange("p a k -> p (a k)")))
                steps.mark(dve.tensor_copy(sel_v[:, bass.ds(h, 1), :].rearrange("p a k -> p (a k)"), top[:, :]))
                settled()
                dve.sem_inc(head_ranked, 1)

            RANK = 18

            def pick(tt):
                steps.then(dve.tensor_copy(gsum[:, :], sel_v[:, :, 0:1].rearrange("p h a -> p (h a)")))
                steps.then(dve.tensor_tensor(sel_v[:, :, :], sel_v[:, :, :],
                                             gsum[:, :].unsqueeze(2).to_broadcast([P, PH, TOPK]), ALU.subtract))
                dve.sem_inc(tops_ready, 1)
                pos = sel_ix[:, :, 2 * TOPK:3 * TOPK]
                steps.mark(dve.tensor_scalar(pos_a[:, :, :], pos, 4, None, ALU.logical_shift_right))
                steps.then(dve.tensor_scalar(pos_b[:, :, :], pos, TOPK - 1, None, ALU.bitwise_and))
                eq4 = eq[:, :, :].rearrange("p (h k) a -> p h k a", h=PH)
                for which, at in ((0, pos_a), (1, pos_b)):
                    steps.then(dve.tensor_tensor(
                        eq[:, :, :],
                        at[:, :, :].rearrange("p h k -> p (h k)").unsqueeze(2).to_broadcast([P, PH * TOPK, TOPK]),
                        iota16[:, :].unsqueeze(1).to_broadcast([P, PH * TOPK, TOPK]), ALU.is_equal))
                    steps.then(dve.tensor_tensor(
                        eq4, eq4,
                        sel_ix[:, :, which * TOPK:(which + 1) * TOPK].unsqueeze(2)
                        .to_broadcast([P, PH, TOPK, TOPK]), ALU.mult))
                    steps.then(dve.tensor_reduce(picked[:, which, :], eq[:, :, :], AX_X, ALU.add))
                dve.wait_ge(exp_done, tt + 1)
                steps.then(dve.tensor_reduce(gsum[:, :], sel_v[:, :, :], AX_X, ALU.add))
                steps.then(dve.reciprocal(gsum[:, :], gsum[:, :]))
                steps.then(dve.tensor_tensor(picked[:, 2, :].rearrange("p (h k) -> p h k", h=PH), sel_v[:, :, :],
                                             gsum[:, :].unsqueeze(2).to_broadcast([P, PH, TOPK]), ALU.mult))
                dve.sem_inc(picked_ready, 1)

            PICK = 13

            with dve.Fori(0, PH) as h:
                inside = steps.enter(h, RANK)
                m = query_scratch(h)
                for s in range(2):
                    dve.wait_ge(scr_drained[s], m.drained(f"s{s}"))
                rank(stage[:, 0, 0:P], stage[:, 1, 0:P], h)
                steps.leave(inside, PH)
            for c in range(2):
                dve.wait_ge(row_hi, 4 * DC + c + 1)
                dve.tensor_tensor(p_lo[:, c, :], p_raw[:, :], p_hi[:, c, :].bitcast(F32), ALU.subtract) \
                    .then_inc(row_lo, 1)
            pick(0)

            def onehots(block4, w, k0):
                dve.wait_ge(gates_filled, block4 + 1)
                for k in range(4):
                    at, col = 4 * w + k, k0 + k
                    steps.mark(dve.tensor_scalar(oh2[:, at, :], iota[:, :], few[:, 1, col:col + 1], None,
                                                 ALU.is_equal))
                    steps.mark(dve.tensor_scalar(oh1h[:, at, :], iota[:, :], few[:, 0, col:col + 1],
                                                 few[:, 2, col:col + 1], ALU.is_equal, ALU.mult))
                    ins = dve.tensor_scalar(oh1l[:, at, :], iota[:, :], few[:, 0, col:col + 1],
                                            few[:, 3, col:col + 1], ALU.is_equal, ALU.mult)
                    if k < 3:
                        steps.mark(ins)
                    else:
                        ins.then_inc(onehot_ready, 1)

            ONEHOTS = 11

            def turn(tt, i, first, last):
                if first:
                    m = select_scratch(tt)
                    dve.wait_ge(scr_filled, m.filled("sel"))
                    steps.mark(dve.tensor_copy(packed[:, 0:2, :].rearrange("p a t -> p (a t)"), scr[1][:, 0:2 * P]))
                    steps.then(dve.tensor_copy(gate_r[:, :], scr[1][:, 2 * P:3 * P]))
                    steps.mark(dve.tensor_copy(packed[:, 2, :], gate_r[:, :].bitcast(F32)))
                    dve.tensor_tensor(packed[:, 3, :], scr[1][:, 2 * P:3 * P], gate_r[:, :].bitcast(F32),
                                      ALU.subtract).then_inc(scr_drained[1], 1)
                    dve.wait_ge(dve_step, steps.n)
                    dve.wait_ge(scr_drained[1], m.drained("sel"))
                dve.wait_ge(dve_step, steps.n)
                dve.wait_ge(onehot_ready, 32 * tt + 8 * i + 1)
                steps.then(dve.tensor_copy(few[:, :, :], packed[:, :, bass.ds(TB * i, TB)]))
                for q in range(4):
                    for w in range(2):
                        onehots(32 * tt + 8 * i + 2 * q + w, w, 8 * q + 4 * w)
                    if q % 2 == 0 and not last:
                        h = 2 * i + q // 2
                        if first and q == 0:
                            dve.wait_ge(score_in, 16 * tt + 16)
                        steps.then(dve.tensor_copy(pair_s[:, :, :], scores[:, bass.ds(2 * h, 2), :]))
                        rank(pair_s[:, 0, :], pair_s[:, 1, :], h)

            TURN = 1 + 8 * ONEHOTS
            RANKS = 2 * (1 + RANK)
            with dve.Fori(0, TT - 1) as tt:
                outer = steps.enter(tt, 3 + 4 * (TURN + RANKS) + PICK)
                turn(tt, 0, True, False)
                with dve.Fori(1, 4) as i:
                    inner = steps.enter(i - 1, TURN + RANKS)
                    turn(tt, i, False, False)
                    steps.leave(inner, 3)
                pick(tt + 1)
                steps.leave(outer, TT - 1)
            turn(TT - 1, 0, True, True)
            with dve.Fori(1, 4) as i:
                inner = steps.enter(i - 1, TURN)
                turn(TT - 1, i, False, True)
                steps.leave(inner, 3)

            def weigh(b):
                dve.wait_ge(gate_ins, 16 * b + 32)
                for k in range(EG):
                    rows = act_in_b[:, k, :].rearrange("p (b t) -> p b t", t=TB)
                    dve.wait_ge(act_in[k], 16 * b + 16)
                    dve.tensor_tensor(rows, rows, gate_in[:, :, k, :], ALU.mult).then_inc(h32_ready, 1)

            def lo_of_round(b, ks):
                for k in ks:
                    dve.wait_ge(hhi_ready, EG * b + k + 1)
                    dve.tensor_tensor(h_lo[:, k, :], act_in_b[:, k, :], h_hi[:, k, :].bitcast(F32), ALU.subtract) \
                        .then_inc(h_ready, 1)

            def sums(b, e):
                for dt in range(DC):
                    dve.wait_ge(b_filled, 16 + 16 * b + 8 * e + dt + 1)
                    dve.wait_ge(b_drained[dt % 4], 4 * b + 2 * e + dt // 4 + 1)
                    dve.tensor_tensor(res[:, dt, :], bslot[dt % 4][:, :], res[:, dt, :], ALU.add) \
                        .then_inc(b_drained[dt % 4], 1)

            weigh(0)
            lo_of_round(0, range(EG))
            with dve.Fori(0, NE // EG - 1) as b:
                sums(b, 0)
                weigh(b + 1)
                lo_of_round(b + 1, (0, 1))
                sums(b, 1)
                lo_of_round(b + 1, (2, 3))
            sums(NE // EG - 1, 0)
            sums(NE // EG - 1, 1)

            for c in range(DC):
                add_square(2 * DC + c, c == 0, c % 2)
            norm_rstd(NORM2, 2)
            norm_rows(4 * DC + 2, 2, a_lo, a_hi)
            steps.then(dve.memset(nt2[:, :], 0.0))
            with dve.Fori(0, DC // 2) as i:
                inside = steps.enter(i, 2)
                for s in range(2):
                    r = res[:, bass.ds(2 * i + s, 1), :].rearrange("p a t -> p (a t)")
                    pl = ple[:, bass.ds(2 * i + s, 1), :].rearrange("p a t -> p (a t)")
                    dve.wait_ge(main_drained[s], F_MAIN + i + 2)
                    steps.then(dve.tensor_tensor(fg[:, s, :], fg[:, s, :], pl, ALU.mult))
                    dve.tensor_tensor(r, r, fg[:, s, :], ALU.add).then_inc(f_added, 1)
                    dve.wait_ge(sq_done, 3 * DC + 2 * i + s + 1)
                    dve.wait_ge(sq_added, 3 * DC + 2 * i + s)
                    dve.tensor_tensor(nt2[:, :], nt2[:, :], sqb[:, s, :], ALU.add).then_inc(sq_added, 1)
                steps.leave(inside, DC // 2)
            norm_rstd(NORM3, 3)
            for c in range(DC):
                dve.scalar_tensor_tensor(res[:, c, :], res[:, c, :], gain[:, 3, c:c + 1], nt0[:, :],
                                         ALU.mult, ALU.mult).then_inc(out_ready, 1)


def weight_tiles(w):
    k, n = w.shape
    return w.reshape(k // P, P, n // P, P).transpose(2, 1, 0, 3).reshape(n // P, P, k)


def shape_constants():
    f = np.float32
    half = DK // 2
    inv = (f(10000.0) ** (-np.arange(half, dtype=f) / f(half))).astype(f)
    ang = (np.arange(T, dtype=f)[None, :] * inv[:, None]).astype(f)
    cos, sin = np.cos(ang).astype(f), np.sin(ang).astype(f)
    rope = np.stack([np.concatenate([cos, cos]), np.concatenate([-sin, sin])])
    scale = f(DK) ** f(-0.5)
    log_gamma = np.log1p(-(f(2.0) ** (f(-5.0) - np.arange(HEADS, dtype=f)))).astype(f)
    pos = np.arange(CHUNK, dtype=f)
    diff = pos[None, :] - pos[:, None]
    head = np.zeros((HEADS, P, 2 * CHUNK + 2), f)
    for h in range(HEADS):
        lg = log_gamma[h]
        head[h, :, 0:CHUNK] = np.where(diff >= 0, np.exp(lg * np.where(diff >= 0, diff, f(0))), f(0)) * scale
        head[h, :, CHUNK:2 * CHUNK] = np.exp(lg * (pos + f(1)))[None, :]
        head[h, :, 2 * CHUNK] = np.exp(lg * (f(CHUNK - 1) - pos)) * scale
        head[h, :, 2 * CHUNK + 1] = np.exp(lg * f(CHUNK))
    shape_c = np.stack([np.eye(P, dtype=f), np.broadcast_to(np.arange(P, dtype=f), (P, P))])
    return rope, head, np.ascontiguousarray(shape_c)


def kernel(x, p, g_mix, w_in, conv_w, conv_b, w_ret_up, w_conv_up, w_out, g_ffn, w_peer_q, peer_k1,
           peer_k2, peer_u, peer_v, g_ple, w_ple_proj, w_ple_gate, g_final):
    import concourse.bacc as bacc
    from concourse.bass_utils import run_bass_kernel_spmd

    def a(v):
        return np.asarray(v)

    w_in_t = weight_tiles(a(w_in)[0])
    at = np.cumsum([0, 4, 4, 8, 8, 8, 8, 8, 8, 8])
    q_, k_, v_, g_, cb, cc, ch, gr, gc = [w_in_t[at[i]:at[i + 1]] for i in range(9)]
    up_r, up_c, w_o = (weight_tiles(a(w)[0]) for w in (w_ret_up, w_conv_up, w_out))
    parts = []
    for h in range(HEADS):
        parts += [k_[h], q_[h], v_[2 * h], v_[2 * h + 1], g_[2 * h], g_[2 * h + 1]]
    for n in range(DC):
        parts += [gr[n], up_r[n]]
    for j in range(DC):
        parts += [cc[j], ch[j], cb[j]]
    for n in range(DC):
        parts += [gc[n], up_c[n]]
    u_tiles = a(peer_u)[0].reshape(NE, P, DC, P).transpose(0, 3, 2, 1).reshape(NE, P, D)
    ple_tiles = weight_tiles(a(w_ple_proj)[0]).reshape(2, 4, P, PLE).transpose(0, 2, 1, 3).reshape(2, P, D)
    stream = np.concatenate([
        np.stack(parts), w_o, weight_tiles(a(w_peer_q)[0]), u_tiles, ple_tiles,
        a(peer_v)[0].reshape(NE, P, D), weight_tiles(a(w_ple_gate)[0])])
    assert stream.shape[0] == 2 * PAIRS
    keys = np.stack([a(peer_k1)[0], a(peer_k2)[0]], 1)
    rope, head_c, shape_c = shape_constants()
    arrays = {
        "x_t": a(x)[0].T,
        "p_t": a(p)[0, 0].T,
        "stream": stream,
        "key_t": keys.transpose(3, 0, 1, 2).reshape(P, 2 * PH, NKEYS),
        "gains": np.stack([a(v).reshape(DC, P) for v in (g_mix, g_ffn, g_ple, g_final)]).transpose(2, 0, 1),
        "conv_c": np.concatenate([a(conv_w)[0], a(conv_b)]).reshape(4, DC, P).transpose(2, 1, 0),
        "rope": rope, "head_c": head_c, "shape_c": shape_c,
    }
    arrays = {k: np.ascontiguousarray(v) for k, v in arrays.items()}
    nc = bacc.Bacc("TRN2", target_bir_lowering=False, num_devices=1)
    ins = [nc.dram_tensor(k, v.shape, F32, kind="ExternalInput").ap() for k, v in arrays.items()]
    out_t = nc.dram_tensor("out_t", (D, T), F32, kind="ExternalOutput").ap()
    score_d = nc.dram_tensor("score_d", (TT, P, 2 * PH, NKEYS), F32, kind="Internal").ap()
    act_d = nc.dram_tensor("act_d", (NE, P, T), F32, kind="Internal").ap()
    gate_d = nc.dram_tensor("gate_d", (T // TB, P, NKEYS, TB), F32, kind="Internal").ap()
    build(nc, *ins, out_t, score_d, act_d, gate_d)
    r = run_bass_kernel_spmd(nc, [arrays], core_ids=[0])
    return np.ascontiguousarray(r.results[0]["out_t"].T)[None]
```

```python
from contextlib import ExitStack

import numpy as np

import concourse.bass as bass
from concourse import mybir

F32 = mybir.dt.float32
F32R = mybir.dt.float32r
BF16 = mybir.dt.bfloat16
U32 = mybir.dt.uint32
ALU = mybir.AluOpType
ACT = mybir.ActivationFunctionType
AX_X = mybir.AxisListType.X

P = 128
D = 1024
T = 1024
DC = D // P
HALF = 512
HEADS, DK, DV = 4, 128, 256
CHUNK = 128
NCH = T // CHUNK
PH, NKEYS, TOPK = 8, 128, 16
TT = T // P
PLE = 256
EPS = 1e-6
LOWEST = -3.0e38
NE = NKEYS

R_PAIR = 0
M1_PAIR = R_PAIR + 3 * HEADS
C_PAIR = M1_PAIR + DC
M2_PAIR = C_PAIR + 3 * DC // 2
O_PAIR = M2_PAIR + DC
Q_PAIR = O_PAIR + DC // 2
A_PAIR = Q_PAIR + PH
P_PAIR = A_PAIR + NE // 2
B_PAIR = P_PAIR + 1
F_PAIR = B_PAIR + NE // 2
PAIRS = F_PAIR + DC // 2
P_MAIN = P_PAIR
F_MAIN = P_MAIN + DC // 2
F_TILE = 2 * B_PAIR

FIRST_QUARTERS = [((), ()), ((), ()), ((), ()), ((), (0,)), ((1,), (2,)), ((3,), (4,)), ((), (5,)), ((), (6,))]
SELECT_AT = 2
TB = 32
OH = 8
EG = 4

FIRST_HEAD = [("kT", 1), ("scores", 0), ("v0", 0), ("v1", 1), ("kv0", 0), ("kv1", 1)]
HEAD = [("o0", 0), ("o1", 1), ("mean", 0), ("kT", 1), ("scores", 0), ("var", 1), ("v0", 0),
        ("v1", 1), ("kv0", 0), ("kv1", 1)]
LAST = [("o0", 0), ("o1", 1), ("mean", 0), ("var", 1)]


class Scratch:

    def __init__(self, uses, filled, before):
        self.uses, self.filled0, self.before = uses, filled, before

    def at(self, name):
        return [n for n, _ in self.uses].index(name)

    def slot(self, name):
        return self.uses[self.at(name)][1]

    def filled(self, name):
        return self.filled0 + self.at(name) + 1

    def free(self, name):
        s = self.slot(name)
        return self.before[s] + sum(1 for _, x in self.uses[:self.at(name)] if x == s) + 1

    def drained(self, name):
        return self.free(name) + 1


def retention_scratch(h):
    if isinstance(h, int) and h == 0:
        return Scratch(FIRST_HEAD, 1, (1, 0))
    uses = LAST if isinstance(h, int) and h == HEADS else HEAD
    return Scratch(uses, 1 + 6 + 10 * (h - 1), (1 + 3 + 5 * (h - 1), 3 + 5 * (h - 1)))


SCRATCH_R = (1 + 3 + 5 * (HEADS - 1) + 2, 3 + 5 * (HEADS - 1) + 2)
FILLED_R = sum(SCRATCH_R)
NORM1 = Scratch([("stat", 0)], FILLED_R, SCRATCH_R)


def query_scratch(h):
    return Scratch([("s0", 0), ("s1", 1)], FILLED_R + 1 + 2 * h, (SCRATCH_R[0] + 1 + h, SCRATCH_R[1] + h))


FILLED_Q = FILLED_R + 1 + 2 * PH


def select_scratch(tt):
    return Scratch([("sel", 1)], FILLED_Q + tt, (0, SCRATCH_R[1] + PH + tt))


FILLED_A = FILLED_Q + TT
NORM2 = Scratch([("stat", 0)], FILLED_A, (SCRATCH_R[0] + 1 + PH, 0))
NORM3 = Scratch([("stat", 0)], FILLED_A + 1, (SCRATCH_R[0] + 2 + PH, 0))


class Steps:

    def __init__(self, eng, sem):
        self.eng, self.sem, self.n, self.k = eng, sem, 0, 0

    def mark(self, ins):
        ins.then_inc(self.sem, 1)
        self.n, self.k = self.n + 1, self.k + 1

    def then(self, ins):
        self.mark(ins)
        self.eng.wait_ge(self.sem, self.n)

    def enter(self, i, per):
        saved = (self.n, self.k)
        self.n, self.k = self.n + i * per, 0
        return saved, per

    def leave(self, entered, turns):
        (n, k), per = entered
        assert self.k == per, (self.k, per)
        self.n, self.k = n + turns * per, k + turns * per


def build(nc, x_t, p_t, stream, key_t, gains, conv_c, rope, head_c, shape_c, out_t,
          score_d, act_d, gate_d):
    with ExitStack() as ctx:
        def sem(name):
            return ctx.enter_context(nc.semaphore(name))

        def psum(name):
            return ctx.enter_context(nc.psum_tensor(name, [P, 2 * HALF], F32))

        base = (nc.sbuf_base + 31) // 32 * 32

        def region(start):
            at = [start]

            def lay(name, shape, dt):
                t = nc.alloc_sbuf_tensor_at(name, shape, dt, offset=at[0])
                size = int(np.prod(shape[1:])) * (2 if dt == BF16 else 4)
                at[0] += (size + 31) // 32 * 32
                return t
            return lay

        K4 = 4096
        set1 = base
        set2 = set1 + 16 * K4
        res0 = set2 + 16 * K4
        ring0 = res0 + 8 * K4
        tmp0 = ring0 + 6 * K4
        const0 = tmp0 + 5 * K4

        lay = region(const0)
        ident = lay("ident", [P, P], F32)
        iota = lay("iota", [P, P], F32)
        iota16 = lay("iota16", [P, TOPK], F32)
        ones_d = lay("ones_d", [P, P], F32)
        ones_v = lay("ones_v", [P, P], F32)
        gain = lay("gain", [P, 4, DC], F32)
        convc = lay("convc", [P, DC, 4], F32)
        eps_t = lay("eps_t", [P, 1], F32)

        lay = region(ring0)
        raw = lay("raw", [P, 2, D], F32)
        w_hi = lay("w_hi", [P, 2, D], F32R)
        w_lo = lay("w_lo", [P, 2, D], F32R)
        lay = region(set1)
        a_hi = lay("a_hi", [P, DC, T], F32R)
        a_lo = lay("a_lo", [P, DC, T], F32R)
        lay = region(set2)
        mix_hi = lay("mix_hi", [P, DC, T], F32R)
        mix_lo = lay("mix_lo", [P, DC, T], F32R)
        lay = region(res0)
        res = lay("res", [P, DC, T], F32)
        lay = region(tmp0)
        nt0 = lay("nt0", [P, T], F32)
        rowb = lay("rowb", [P, 4, T], F32)
        sqb = rowb[:, 0:2, :]
        nt1 = rowb[:, 2, :]
        nt2 = rowb[:, 3, :]
        lay = region(tmp0)
        sg = lay("sg", [P, T], F32)
        pbuf = lay("pbuf", [P, T + 2], F32)
        z = lay("z", [P, T], F32)
        lay = region(tmp0)
        p_hi = lay("p_hi", [P, 2, T], F32R)
        p_lo = lay("p_lo", [P, 2, T], F32R)
        p_raw = lay("p_raw", [P, T], F32)
        lay = region(set2)
        cos = lay("cos", [P, T], F32)
        sin = lay("sin", [P, T], F32)
        kT = lay("kT", [P, T], F32)
        qT = lay("qT", [P, T], F32)
        swapped = lay("swapped", [P, T], F32)
        vrow = lay("vrow", [P, T], F32)
        ktok = lay("ktok", [P, NCH, DK], F32)
        vtok = lay("vtok", [P, NCH, DV], F32)
        sdec = lay("sdec", [P, NCH, CHUNK], F32)
        state = lay("state", [P, NCH - 1, DV], F32)
        headc = lay("headc", [P, 2 * CHUNK], F32)
        y = lay("y", [P, 2, T], F32)
        g = lay("g", [P, 2, T], F32)
        headz = nc.alloc_sbuf_tensor_at("headz", [P, 2], F32, offset=const0 + 2560 + 512)
        xi = headc[:, CHUNK:2 * CHUNK]
        lay = region(set1)
        scores = lay("scores", [P, PH * 2, NKEYS], F32)
        gbuf = lay("gbuf", [P, NKEYS, TB], F32)
        actb = lay("actb", [P, 2, T], F32)
        hot = lay("hot", [P, 2, 2, 4, NKEYS], F32R)
        oh1 = lay("oh1", [P, OH, 2, NKEYS], F32R)
        eq = lay("eq", [P, PH * TOPK, TOPK], BF16)
        pair_s = lay("pair_s", [P, 2, NKEYS], F32)
        candl = pair_s[:, :, :].rearrange("p a n -> p (a n)")
        left = lay("left", [P, 2, NKEYS], F32)
        cand = lay("cand", [P, TOPK, TOPK], F32)
        v16 = lay("v16", [P, 2, TOPK], F32)
        ix = lay("ix", [P, 3, TOPK], U32)
        top = lay("top", [P, TOPK], F32)
        sel_ix = lay("sel_ix", [P, PH, 3 * TOPK], U32)
        sel_v = lay("sel_v", [P, PH, TOPK], F32)
        pos_a = lay("pos_a", [P, PH, TOPK], U32)
        pos_b = lay("pos_b", [P, PH, TOPK], U32)
        picked = lay("picked", [P, 3, P], F32)
        gsum = lay("gsum", [P, PH], F32)
        packed = lay("packed", [P, 4, P], F32)
        gate_r = lay("gate_r", [P, P], F32R)
        few = lay("few", [P, 4, TB], F32)
        lay = region(set1 + 2 * K4)
        qrow = lay("qrow", [P, 2, T], F32)
        stage = lay("stage", [P, 2, T], F32)
        keys = lay("keys", [P, 2 * PH, NKEYS], F32)
        lay = region(set1)
        h_hi = lay("h_hi", [P, EG, T], F32R)
        h_lo = lay("h_lo", [P, EG, T], F32R)
        act_in_b = lay("act_in_b", [P, EG, T], F32)
        gate_in = lay("gate_in", [P, T // TB, EG, TB], F32)
        v_hi = lay("v_hi", [P, EG, D], F32R)
        v_lo = lay("v_lo", [P, EG, D], F32R)
        ple = lay("ple", [P, DC, T], F32)
        lay = region(set2)
        fg = lay("fg", [P, 2, T], F32)

        main = [psum("main0"), psum("main1")]
        scr = [psum("scr0"), psum("scr1")]
        bslot = main + scr

        raw_in = [sem("raw_in0"), sem("raw_in1")]
        hi_made = sem("hi_made")
        tile_split = sem("tile_split")
        tile_done = sem("tile_done")
        main_drained = [sem("main_drained0"), sem("main_drained1")]
        scr_filled = sem("scr_filled")
        scr_drained = [sem("scr_drained0"), sem("scr_drained1")]
        consts_in = sem("consts_in")
        rope_in = sem("rope_in")
        x_in = [sem(f"x_in{c}") for c in range(DC)]
        ones_set = sem("ones_set")
        sq_done = sem("sq_done")
        sq_added = sem("sq_added")
        std_done = sem("std_done")
        row_made = sem("row_made")
        row_hi = sem("row_hi")
        row_lo = sem("row_lo")
        norm_lo = [sem("norm_lo_dve"), sem("norm_lo_pool")]
        dve_step = sem("dve_step")
        headc_in = sem("headc_in")
        kq_ready = sem("kq_ready")
        qxi_ready = sem("qxi_ready")
        states_ready = sem("states_ready")
        ysum_ready = sem("ysum_ready")
        centered = sem("centered")
        ysq_ready = sem("ysq_ready")
        ysqsum_ready = sem("ysqsum_ready")
        gstd_done = sem("gstd_done")
        ret_ready = sem("ret_ready")
        sig_ready = sem("sig_ready")
        merged_done = sem("merged_done")
        z_ready = sem("z_ready")
        z_hi = sem("z_hi")
        z_used = sem("z_used")
        keys_in = sem("keys_in")
        score_st = [sem("score_st0"), sem("score_st1")]
        score_in = sem("score_in")
        head_ranked = sem("head_ranked")
        tops_ready = sem("tops_ready")
        exp_done = sem("exp_done")
        picked_ready = sem("picked_ready")
        hot_made = sem("hot_made")
        oh_hi_ready = sem("oh_hi_ready")
        oh_lo_ready = sem("oh_lo_ready")
        gates_filled = sem("gates_filled")
        gates_drained = sem("gates_drained")
        act_st = [sem("act_st0"), sem("act_st1")]
        gate_st = sem("gate_st")
        p_in = sem("p_in")
        ple_filled = sem("ple_filled")
        v_hi_made = sem("v_hi_made")
        v_split = sem("v_split")
        act_in = [sem(f"act_in{k}") for k in range(EG)]
        gate_ins = sem("gate_ins")
        h32_ready = sem("h32_ready")
        hhi_ready = sem("hhi_ready")
        h_ready = sem("h_ready")
        b_filled = sem("b_filled")
        b_drained = [sem(f"b_drained{k}") for k in range(4)]
        f_added = sem("f_added")
        out_ready = sem("out_ready")
        out_st = sem("out_st")
        passed = sem("passed")
        passed_pool = sem("passed_pool")

        block = ctx.enter_context(nc.Block())

        @block.sync
        def _(sp):
            def load(pair, s):
                sp.dma_start(raw[:, s, :], stream[bass.ds(2 * pair + s, 1)].rearrange("a p n -> p (a n)")) \
                    .then_inc(raw_in[s], 16)

            for c in range(DC):
                sp.dma_start(res[:, c, :], x_t[c * P:(c + 1) * P, :]).then_inc(x_in[c], 16)
            load(0, 0)
            sp.dma_start(gain[:, :, :], gains).then_inc(consts_in, 16)
            load(0, 1)
            sp.dma_start(ident[:, :], shape_c[0]).then_inc(consts_in, 16)
            sp.dma_start(iota[:, :], shape_c[1]).then_inc(consts_in, 16)
            sp.dma_start(iota16[:, :], shape_c[1, :, 0:TOPK]).then_inc(consts_in, 16)
            sp.dma_start(convc[:, :, :], conv_c).then_inc(consts_in, 16)
            sp.dma_start(cos[:, :], rope[0]).then_inc(rope_in, 16)
            sp.dma_start(sin[:, :], rope[1]).then_inc(rope_in, 16)
            with sp.Fori(1, B_PAIR) as pair:
                for s in range(2):
                    sp.wait_ge(tile_split, 2 * pair + s - 1)
                    load(pair, s)

            for s in range(2):
                sp.wait_ge(tile_split, 2 * B_PAIR + s - 1)
                load(B_PAIR, s)
            with sp.Fori(1, NE // 2) as i:
                for s in range(2):
                    sp.wait_ge(v_split, 2 * i + s - 1)
                    load(B_PAIR + i, s)
            for s in range(2):
                sp.wait_ge(v_split, NE + s - 1)
                load(F_PAIR, s)
            with sp.Fori(1, DC // 2) as i:
                for s in range(2):
                    sp.wait_ge(tile_split, F_TILE + 2 * i + s - 1)
                    load(F_PAIR + i, s)
            for c in range(DC):
                sp.wait_ge(out_ready, c + 1)
                sp.dma_start(out_t[c * P:(c + 1) * P, :], res[:, c, :]).then_inc(out_st, 16)
            sp.wait_ge(out_st, 16 * DC)

        @block.gpsimd
        def _(pool):
            def split(pair, s, tile, peeled):
                pool.wait_ge(raw_in[s], 16 * pair + 16)
                if not peeled:
                    pool.wait_ge(tile_done, tile - 1)
                pool.sem_inc(passed_pool, 1)
                pool.tensor_copy(w_hi[:, s, :], raw[:, s, :]).then_inc(hi_made, 1)
                pool.wait_ge(hi_made, tile + 1)
                pool.tensor_tensor(w_lo[:, s, :], raw[:, s, :], w_hi[:, s, :].bitcast(F32), ALU.subtract) \
                    .then_inc(tile_split, 1)

            def odd_rows(norm, first, dst_lo, dst_hi):
                for c in range(1, DC, 2):
                    pool.wait_ge(row_hi, first + c + 1)
                    pool.tensor_tensor(dst_lo[:, c, :], rowb[:, c % 4, :], dst_hi[:, c, :].bitcast(F32),
                                       ALU.subtract).then_inc(norm_lo[1], 1)

            split(0, 0, 0, True)
            split(0, 1, 1, True)
            odd_rows(0, 0, a_lo, a_hi)
            with pool.Fori(1, Q_PAIR + 1) as pair:
                for s in range(2):
                    split(pair, s, 2 * pair + s, False)
            odd_rows(1, 3 * DC, mix_lo, mix_hi)
            with pool.Fori(Q_PAIR + 1, B_PAIR) as pair:
                for s in range(2):
                    split(pair, s, 2 * pair + s, False)
            pool.wait_ge(tile_done, 2 * A_PAIR + NE)
            with pool.Fori(0, NE // EG) as b:
                for k in range(EG):
                    s = k % 2
                    pool.wait_ge(raw_in[s], 16 * (B_PAIR + 2 * b + k // 2) + 16)
                    pool.wait_ge(b_filled, 16 * b + 8 * (k // 2) + 8)
                    pool.sem_inc(passed_pool, 1)
                    pool.tensor_copy(v_hi[:, k, :], raw[:, s, :]).then_inc(v_hi_made, 1)
                    pool.wait_ge(v_hi_made, EG * b + k + 1)
                    pool.tensor_tensor(v_lo[:, k, :], raw[:, s, :], v_hi[:, k, :].bitcast(F32), ALU.subtract) \
                        .then_inc(v_split, 1)
            for s in range(2):
                split(F_PAIR, s, F_TILE + s, False)
            odd_rows(2, 4 * DC + 2, a_lo, a_hi)
            with pool.Fori(1, DC // 2) as i:
                for s in range(2):
                    split(F_PAIR + i, s, F_TILE + 2 * i + s, False)

        @block.tensor
        def _(pe):
            def tile_mm(tile, use, s, rhs_hi, rhs_lo, ready=None, norm=None, amid=None):
                pe.wait_ge(tile_split, tile + 1)
                pe.wait_ge(main_drained[s], use + 1)
                for c in range(DC):
                    if ready is not None:
                        pe.wait_ge(row_lo, ready + c + 1)
                    if norm is not None:
                        pe.wait_ge(norm_lo[c % 2], 4 * norm + c // 2 + 1)
                    if amid is not None and c == DC // 2:
                        amid()
                    for wt, rows in ((w_hi, rhs_hi), (w_hi, rhs_lo), (w_lo, rhs_hi)):
                        for half in range(2):
                            last = pe.matmul(main[s][:, half * HALF:(half + 1) * HALF],
                                             wt[:, s, c * P:(c + 1) * P],
                                             rows[:, c, half * HALF:(half + 1) * HALF],
                                             start=(c == 0 and wt is w_hi and rows is rhs_hi),
                                             stop=(c == DC - 1 and wt is w_lo))
                last.then_inc(tile_done, 1)

            def fill(m, name):
                pe.wait_ge(scr_drained[m.slot(name)], m.free(name))
                return scr[m.slot(name)]

            def column_mean(m, name, ones, rows):
                slot = fill(m, name)
                for half in range(2):
                    last = pe.matmul(slot[:, half * HALF:(half + 1) * HALF], ones[:, :],
                                     rows[:, half * HALF:(half + 1) * HALF], start=True, stop=True)
                last.then_inc(scr_filled, 1)

            for q in (main_drained[0], main_drained[1], scr_drained[0], scr_drained[1]):
                pe.sem_inc(q, 1)
            for q in b_drained:
                pe.sem_inc(q, 1)
            pe.sem_inc(gates_drained, 2)
            pe.sem_inc(gates_filled, 2)
            pe.sem_inc(b_filled, 16)

            pe.wait_ge(ones_set, 3)
            pe.wait_ge(sq_added, DC)
            column_mean(Scratch([("stat", 0)], 0, (0, 0)), "stat", ones_d, nt2)
            pe.wait_ge(consts_in, 16 * 5)

            def out_part(m, h, e):
                slot = fill(m, f"o{e}")
                for n in range(NCH):
                    dst = slot[:, n * CHUNK:(n + 1) * CHUNK]
                    last = pe.matmul(dst, vtok[:, n, e * P:(e + 1) * P], sdec[:, n, :],
                                     start=True, stop=(n == 0))
                    if n:
                        last = pe.matmul(dst, state[:, n - 1, e * P:(e + 1) * P],
                                         qT[:, n * CHUNK:(n + 1) * CHUNK], start=False, stop=True)
                last.then_inc(scr_filled, 1)

            def to_tokens(m, name, rows):
                slot = fill(m, name)
                for n in range(NCH):
                    last = pe.transpose(slot[:, n * P:(n + 1) * P], rows[:, n * P:(n + 1) * P], ident[:, :])
                last.then_inc(scr_filled, 1)

            def head(h, first=False):
                m = retention_scratch(h)
                tile, use = 6 * h, 3 * h
                tile_mm(tile, use, 0, a_hi, a_lo, norm=0 if first else None)
                if not first:
                    pe.wait_ge(states_ready, h)
                    pe.wait_ge(scr_drained[0], m.free("o0"))
                    out_part(m, h, 0)
                tile_mm(tile + 1, use, 1, a_hi, a_lo)
                if not first:
                    out_part(m, h, 1)
                tile_mm(tile + 2, use + 1, 0, a_hi, a_lo)
                if not first:
                    pe.wait_ge(ysum_ready, h)
                    column_mean(m, "mean", ones_v, nt2)
                pe.wait_ge(kq_ready, 2 * h + 1)
                to_tokens(m, "kT", kT)
                pe.wait_ge(kq_ready, 2 * h + 2)
                slot = fill(m, "scores")
                for n in range(NCH):
                    c = slice(n * CHUNK, (n + 1) * CHUNK)
                    last = pe.matmul(slot[:, c], kT[:, c], qT[:, c], start=True, stop=True)
                last.then_inc(scr_filled, 1)
                tile_mm(tile + 3, use + 1, 1, a_hi, a_lo)
                if not first:
                    pe.wait_ge(ysqsum_ready, h)
                    column_mean(m, "var", ones_v, nt2)
                pe.wait_ge(main_drained[0], use + 3)
                to_tokens(m, "v0", vrow)
                tile_mm(tile + 4, use + 2, 0, a_hi, a_lo)
                pe.wait_ge(main_drained[1], use + 3)
                to_tokens(m, "v1", vrow)
                tile_mm(tile + 5, use + 2, 1, a_hi, a_lo)
                pe.wait_ge(scr_drained[1], m.drained("v1"))
                for e, ns in ((0, range(0, 4)), (1, range(4, NCH - 1))):
                    slot = fill(m, f"kv{e}")
                    for n in ns:
                        last = pe.matmul(slot[:, (n - 4 * e) * DV:(n - 4 * e + 1) * DV], ktok[:, n, :],
                                         vtok[:, n, :], start=True, stop=True)
                    last.then_inc(scr_filled, 1)

            head(0, True)
            with pe.Fori(1, HEADS) as h:
                head(h)
            m = retention_scratch(HEADS)
            pe.wait_ge(states_ready, HEADS)
            out_part(m, HEADS, 0)
            out_part(m, HEADS, 1)
            pe.wait_ge(ysum_ready, HEADS)
            column_mean(m, "mean", ones_v, nt2)

            def variance():
                pe.wait_ge(ysqsum_ready, HEADS)
                column_mean(m, "var", ones_v, nt2)

            tile_mm(2 * M1_PAIR, M1_PAIR, 0, a_hi, a_lo, amid=variance)
            tile_mm(2 * M1_PAIR + 1, M1_PAIR, 1, mix_hi, mix_lo, ready=0)
            with pe.Fori(1, DC) as n:
                tile_mm(2 * (M1_PAIR + n), M1_PAIR + n, 0, a_hi, a_lo)
                tile_mm(2 * (M1_PAIR + n) + 1, M1_PAIR + n, 1, mix_hi, mix_lo)
            with pe.Fori(0, DC // 2) as i:
                for k in range(6):
                    pair = C_PAIR + 3 * i + k // 2
                    tile_mm(2 * pair + k % 2, pair, k % 2, a_hi, a_lo)
            tile_mm(2 * M2_PAIR, M2_PAIR, 0, a_hi, a_lo)
            pe.wait_ge(z_used, DC + 1)
            tile_mm(2 * M2_PAIR + 1, M2_PAIR, 1, mix_hi, mix_lo)
            with pe.Fori(1, DC) as n:
                tile_mm(2 * (M2_PAIR + n), M2_PAIR + n, 0, a_hi, a_lo)
                tile_mm(2 * (M2_PAIR + n) + 1, M2_PAIR + n, 1, mix_hi, mix_lo)
            with pe.Fori(0, DC // 2) as i:
                for s in range(2):
                    tile_mm(2 * (O_PAIR + i) + s, O_PAIR + i, s, a_hi, a_lo, ready=DC if s == 0 else None)
            pe.wait_ge(sq_added, 2 * DC)
            column_mean(NORM1, "stat", ones_d, nt2)

            def key_scores(h, s):
                m = query_scratch(h)
                pe.wait_ge(main_drained[s], Q_PAIR + h + 2)
                slot = fill(m, f"s{s}")
                for t in range(TT):
                    last = pe.matmul(slot[:, t * P:(t + 1) * P], qrow[:, s, t * P:(t + 1) * P],
                                     keys[:, bass.ds(2 * h + s, 1), :].rearrange("p a n -> p (a n)"),
                                     start=True, stop=True)
                last.then_inc(scr_filled, 1)

            def queries(h, first=False):
                tile_mm(2 * (Q_PAIR + h), Q_PAIR + h, 0, mix_hi, mix_lo, norm=1 if first else None)
                if not first:
                    key_scores(h - 1, 1)
                tile_mm(2 * (Q_PAIR + h) + 1, Q_PAIR + h, 1, mix_hi, mix_lo)
                key_scores(h, 0)

            pe.wait_ge(keys_in, 16)
            queries(0, True)
            with pe.Fori(1, PH) as h:
                queries(h)
            key_scores(PH - 1, 1)

            def quarter(m, sel=None):
                for w in range(2):
                    pe.wait_ge(oh_hi_ready, 2 * m + w + 2)
                    pe.wait_ge(oh_lo_ready, 2 * m + w + 2)
                    pe.wait_ge(gates_drained, 2 * m + w + 1)
                    if w and sel is not None:
                        pe.wait_ge(scr_drained[1], sel.drained("sel"))
                    for k in range(4):
                        last = pe.matmul(scr[w][:, 2 * k * P:2 * (k + 1) * P], hot[:, w, 1, k, :],
                                         oh1[:, 4 * w + k, :, :].rearrange("p a n -> p (a n)"),
                                         start=True, stop=True)
                    last.then_inc(gates_filled, 1)

            def select(tt, first=False):
                m = select_scratch(tt)
                pe.wait_ge(picked_ready, tt + 1)
                if not first:
                    pe.wait_ge(gates_drained, 32 * tt)
                slot = fill(m, "sel")
                for k in range(3):
                    last = pe.transpose(slot[:, k * P:(k + 1) * P], picked[:, k, :], ident[:, :])
                last.then_inc(scr_filled, 1)
                return m

            def expert_tile(tt, i, q, amid=None):
                pair = A_PAIR + 8 * tt + 2 * i + q // 2
                tile_mm(2 * pair + q % 2, pair, q % 2, mix_hi, mix_lo, amid=amid)

            pe.wait_ge(scr_drained[0], query_scratch(PH - 1).drained("s0"))
            for n, (amid, ms) in enumerate(FIRST_QUARTERS):
                expert_tile(0, n // 4, n % 4, amid=lambda: [quarter(m) for m in amid])
                if n == SELECT_AT:
                    sel0 = select(0, True)
                for m in ms:
                    quarter(m, sel=sel0)
            with pe.Fori(2, 4) as i:
                for q in range(4):
                    expert_tile(0, i, q)
                    quarter(4 * i + q - 1)
            with pe.Fori(1, TT) as tt:
                for q in range(4):
                    expert_tile(tt, 0, q)
                    sel = select(tt) if q == 0 else None
                    quarter(16 * tt + q - 1, sel=sel)
                with pe.Fori(1, 4) as i:
                    for q in range(4):
                        expert_tile(tt, i, q)
                        quarter(16 * tt + 4 * i + q - 1)

            for n in range(DC):
                s = n % 2
                if n % 4 == 0:
                    pe.wait_ge(tile_split, 2 * P_PAIR + n // 4 + 1)
                    pe.wait_ge(row_lo, 2 * DC + 2)
                pe.wait_ge(main_drained[s], P_MAIN + n // 2 + 1)
                for c in range(2):
                    col = (n % 4 * 2 + c) * P
                    for wt, rows in ((w_hi, p_hi), (w_hi, p_lo), (w_lo, p_hi)):
                        for half in range(2):
                            last = pe.matmul(main[s][:, half * HALF:(half + 1) * HALF],
                                             wt[:, n // 4, col:col + P], rows[:, c, half * HALF:(half + 1) * HALF],
                                             start=(c == 0 and wt is w_hi and rows is p_hi),
                                             stop=(c == 1 and wt is w_lo))
                last.then_inc(tile_done if n % 4 == 3 else ple_filled, 1)
                if n == 1:
                    quarter(NE - 1)

            def pairs_of_experts(b):
                for e in range(2):
                    pe.wait_ge(v_split, EG * b + 2 * e + 2)
                    pe.wait_ge(h_ready, EG * b + 2 * e + 2)
                    for dt in range(DC):
                        slot = bslot[dt % 4]
                        pe.wait_ge(b_drained[dt % 4], 4 * b + 2 * e + dt // 4 + 1)
                        for k in (2 * e, 2 * e + 1):
                            for vt, ht in ((v_hi, h_hi), (v_hi, h_lo), (v_lo, h_hi)):
                                for half in range(2):
                                    last = pe.matmul(slot[:, half * HALF:(half + 1) * HALF],
                                                     vt[:, k, dt * P:(dt + 1) * P],
                                                     ht[:, k, half * HALF:(half + 1) * HALF],
                                                     start=(k % 2 == 0 and vt is v_hi and ht is h_hi),
                                                     stop=(k % 2 == 1 and vt is v_lo))
                        last.then_inc(b_filled, 1)

            for s in range(2):
                pe.wait_ge(main_drained[s], F_MAIN + 1)
            pe.wait_ge(gates_drained, 2 + T // 4)
            pe.wait_ge(scr_drained[1], select_scratch(TT - 1).drained("sel"))
            with pe.Fori(0, NE // EG) as b:
                pairs_of_experts(b)

            pe.wait_ge(sq_added, 3 * DC)
            column_mean(NORM2, "stat", ones_d, nt2)
            with pe.Fori(0, DC // 2) as i:
                for s in range(2):
                    tile_mm(F_TILE + 2 * i + s, F_MAIN + i, s, a_hi, a_lo, norm=2 if s == 0 else None)
            pe.wait_ge(sq_added, 4 * DC)
            column_mean(NORM3, "stat", ones_d, nt2)

        @block.scalar
        def _(act):
            def square(i, src, peeled=False):
                if not peeled:
                    act.wait_ge(sq_added, i - 1)
                act.activation(sqb[:, i % 2, :] if isinstance(i, int) else None, src, ACT.Square) \
                    .then_inc(sq_done, 1)

            def rough_rstd(slot, done, count):
                act.activation(nt0[:, :], slot[:, :], ACT.Ln, bias=eps_t[:, 0:1]).then_inc(done, 1)
                act.wait_ge(done, count + 1)
                act.activation(nt0[:, :], nt0[:, :], ACT.Exp, scale=-0.5).then_inc(done, 1)

            def norm_std(m, count):
                act.wait_ge(scr_filled, m.filled("stat"))
                rough_rstd(scr[0], std_done, 2 * count)

            def hi_rows(dst, norm):
                for c in range(DC):
                    act.wait_ge(row_made, norm * DC + c + 1)
                    act.copy(dst[:, c, :], rowb[:, c % 4, :]).then_inc(row_hi, 1)

            act.sem_inc(act_st[0], 16)
            act.sem_inc(act_st[1], 16)
            act.sem_inc(gate_st, 16)
            act.sem_inc(score_st[0], 16)
            act.sem_inc(score_st[1], 16)

            act.wait_ge(ones_set, 3)
            for c in range(DC):
                act.wait_ge(x_in[c], 16)
                square(c, res[:, c, :], peeled=c < 2)
            act.dma_start(headc[:, :], head_c[0, :, 0:2 * CHUNK]).then_inc(headc_in, 16)
            act.dma_start(headz[:, :], head_c[0, :, 2 * CHUNK:2 * CHUNK + 2]).then_inc(headc_in, 16)
            norm_std(Scratch([("stat", 0)], 0, (0, 0)), 0)
            hi_rows(a_hi, 0)

            def ret_hi(cs):
                for c in cs:
                    act.wait_ge(ret_ready, 2 * (c // 2) + 3)
                    act.copy(mix_hi[:, c, :], res[:, c, :]).then_inc(row_hi, 1)

            def head(h, first=False, last=False):
                m = retention_scratch(h)
                if not first:
                    for e in range(2):
                        act.wait_ge(scr_filled, m.filled(f"o{e}"))
                        act.wait_ge(ret_ready, 2 * h - 1)
                        act.copy(y[:, e, :], scr[e][:, :]).then_inc(scr_drained[e], 1)
                if last:
                    ret_hi(range(0, 3))
                if not last:
                    if not first:
                        act.wait_ge(states_ready, h)
                        hc = head_c[bass.ds(h, 1)].rearrange("a p n -> p (a n)")
                        act.dma_start(headc[:, :], hc[:, 0:2 * CHUNK]).then_inc(headc_in, 16)
                        act.dma_start(headz[:, :], hc[:, 2 * CHUNK:2 * CHUNK + 2]).then_inc(headc_in, 16)
                    act.wait_ge(tile_done, 6 * h + 3)
                    act.copy(vrow[:, :], main[0][:, :]).then_inc(main_drained[0], 1)
                if not first:
                    for e in range(2):
                        act.wait_ge(centered, 2 * h - 1 + e)
                        act.activation(sqb[:, e, :], y[:, e, :], ACT.Square).then_inc(ysq_ready, 1)
                if last:
                    ret_hi(range(3, 4))
                if not last:
                    act.wait_ge(scr_filled, m.filled("kT"))
                    act.wait_ge(headc_in, 32 * h + 32)
                    act.activation(ktok[:, :, :].rearrange("p n k -> p (n k)"), scr[1][:, :], ACT.Copy,
                                   scale=headz[:, 0:1]).then_inc(scr_drained[1], 1)
                if not first:
                    act.wait_ge(scr_filled, m.filled("var"))
                    rough_rstd(scr[1], gstd_done, 2 * (h - 1))
                if not last:
                    act.wait_ge(scr_filled, m.filled("v0"))
                    act.copy(vtok[:, :, 0:P], scr[0][:, :].rearrange("p (n k) -> p n k", n=NCH)) \
                        .then_inc(scr_drained[0], 1)
                    act.wait_ge(tile_done, 6 * h + 4)
                    act.copy(vrow[:, :], main[1][:, :]).then_inc(main_drained[1], 1)
                    act.wait_ge(tile_done, 6 * h + 5)
                    if not first:
                        act.wait_ge(ret_ready, 2 * h + 1)
                    act.activation(g[:, 0, :], main[0][:, :], ACT.Sigmoid).then_inc(sig_ready, 1)
                    act.wait_ge(scr_filled, m.filled("v1"))
                    act.copy(vtok[:, :, P:DV], scr[1][:, :].rearrange("p (n k) -> p n k", n=NCH)) \
                        .then_inc(scr_drained[1], 1)
                    act.wait_ge(tile_done, 6 * h + 6)
                    act.activation(g[:, 1, :], main[1][:, :], ACT.Sigmoid).then_inc(sig_ready, 1)

            head(0, first=True)
            with act.Fori(1, HEADS) as h:
                head(h)
            head(HEADS, last=True)
            ret_hi(range(4, DC))

            with act.Fori(0, DC) as n:
                act.wait_ge(tile_done, 2 * (M1_PAIR + n) + 1)
                act.wait_ge(merged_done, n + 1)
                act.activation(sg[:, :], main[0][:, :], ACT.Sigmoid).then_inc(main_drained[0], 1)
            with act.Fori(0, DC // 2) as i:
                for k in range(2):
                    pair = C_PAIR + 3 * i + (3 * k) // 2
                    s = k
                    act.wait_ge(tile_done, 2 * pair + s + 1)
                    act.wait_ge(merged_done, DC + 2 * i + k + 1)
                    act.copy(sg[:, :], main[s][:, :]).then_inc(main_drained[s], 1)
                    act.wait_ge(z_ready, 2 * i + k + 1)
                    act.copy(mix_hi[:, bass.ds(2 * i + k, 1), :].rearrange("p a t -> p (a t)"), z[:, :]) \
                        .then_inc(z_hi, 1)
            with act.Fori(0, DC) as n:
                act.wait_ge(tile_done, 2 * (M2_PAIR + n) + 1)
                act.wait_ge(merged_done, 2 * DC + n + 1)
                act.activation(sg[:, :], main[0][:, :], ACT.Sigmoid).then_inc(main_drained[0], 1)
            for c in range(DC):
                act.wait_ge(merged_done, 2 * DC + c + 2)
                act.copy(a_hi[:, c, :], res[:, c, :]).then_inc(row_hi, 1)
            for c in range(DC):
                act.wait_ge(row_lo, DC + c + 1)
                act.dma_start(res[:, c, :], x_t[c * P:(c + 1) * P, :]).then_inc(x_in[c], 16)
            with act.Fori(0, DC // 2) as i:
                for s in range(2):
                    act.wait_ge(main_drained[s], O_PAIR + i + 2)
                    act.wait_ge(sq_added, DC + 2 * i + s - 1)
                    act.activation(sqb[:, s, :], res[:, bass.ds(2 * i + s, 1), :].rearrange("p a t -> p (a t)"),
                                   ACT.Square).then_inc(sq_done, 1)
            norm_std(NORM1, 1)
            act.dma_start(keys[:, :, :], key_t).then_inc(keys_in, 16)
            hi_rows(mix_hi, 1)

            for c in range(2):
                if c == 0:
                    for q in norm_lo:
                        act.wait_ge(q, 4 * 2)
                act.wait_ge(row_lo, 2 * DC + c)
                act.dma_start(p_raw[:, :], p_t[c * P:(c + 1) * P, :]).then_inc(p_in, 16)
                act.wait_ge(p_in, 16 * c + 16)
                act.copy(p_hi[:, c, :], p_raw[:, :]).then_inc(row_hi, 1)

            def query(h, s):
                act.wait_ge(tile_done, 2 * (Q_PAIR + h) + s + 1)
                act.copy(qrow[:, s, :], main[s][:, :]).then_inc(main_drained[s], 1)

            def scores_out(h, s):
                m = query_scratch(h)
                act.wait_ge(scr_filled, m.filled(f"s{s}"))
                act.wait_ge(score_st[s], 16 * h + 16)
                act.wait_ge(head_ranked, h + 1)
                act.copy(stage[:, s, :], scr[s][:, :]).then_inc(scr_drained[s], 1)
                act.wait_ge(scr_drained[s], m.drained(f"s{s}"))
                act.dma_start(score_d[:, :, bass.ds(2 * h + s, 1), :].rearrange("t p a n -> p t (a n)"),
                              stage[:, s, :].rearrange("p (t n) -> p t n", t=TT)).then_inc(score_st[s], 16)

            query(0, 0)
            query(0, 1)
            scores_out(0, 0)
            with act.Fori(1, PH) as h:
                query(h, 0)
                scores_out(h - 1, 1)
                query(h, 1)
                scores_out(h, 0)
            scores_out(PH - 1, 1)

            def softmax(tt):
                act.wait_ge(tops_ready, tt + 1)
                act.activation(sel_v[:, :, :], sel_v[:, :, :], ACT.Exp).then_inc(exp_done, 1)

            softmax(0)
            for s in range(2):
                act.wait_ge(score_st[s], 16 * PH + 16)

            def load_scores(tt):
                act.wait_ge(head_ranked, PH * tt + 1)
                act.dma_start(scores[:, :, :], score_d[bass.ds(tt, 1)].rearrange("a p h n -> p (a h) n")) \
                    .then_inc(score_in, 16)

            def store_gates(m, block):
                act.wait_ge(gates_drained, 2 * m + 4)
                act.dma_start(gate_d[bass.ds(block, 1)].rearrange("a p e t -> p (a e t)"),
                              gbuf[:, :, :].rearrange("p e t -> p (e t)")).then_inc(gate_st, 16)

            def hi_of_gates(m, mq):
                for w in range(2):
                    act.wait_ge(hot_made, 2 * m + w + 1)
                    for k in range(4):
                        col = 8 * mq + 4 * w + k
                        ins = act.activation(oh1[:, 4 * w + k, 0, :], hot[:, w, 0, k, :].bitcast(F32), ACT.Copy,
                                             scale=few[:, 2, col:col + 1])
                    ins.then_inc(oh_hi_ready, 1)

            def expert_tile(tt, i, q, quarters=None):
                pair = A_PAIR + 8 * tt + 2 * i + q // 2
                s = q % 2
                act.wait_ge(tile_done, 2 * pair + s + 1)
                act.wait_ge(act_st[s], 16 * (8 * tt + 2 * i + q // 2) + 16)
                act.activation(actb[:, s, :], main[s][:, :], ACT.Gelu).then_inc(main_drained[s], 1)
                act.wait_ge(main_drained[s], pair + 2)
                act.dma_start(act_d[bass.ds(16 * tt + 4 * i + q, 1)].rearrange("a p n -> p (a n)"),
                              actb[:, s, :]).then_inc(act_st[s], 16)
                if quarters is None:
                    if q == 0:
                        store_gates(16 * tt + 4 * i - 1, 4 * tt + i - 1)
                    hi_of_gates(16 * tt + 4 * i + q, q)
                else:
                    for m in quarters:
                        if m % 4 == 3:
                            store_gates(m, m // 4)
                        hi_of_gates(m + 1, (m + 1) % 4)

            load_scores(1)
            for n, (amid, ms) in enumerate(FIRST_QUARTERS):
                for m in amid:
                    if m % 4 == 3:
                        store_gates(m, m // 4)
                    hi_of_gates(m + 1, (m + 1) % 4)
                expert_tile(0, n // 4, n % 4, quarters=ms)
                if n == SELECT_AT:
                    hi_of_gates(0, 0)
            for q in range(4):
                expert_tile(0, 2, q)
            for q in range(4):
                if q == 1:
                    softmax(1)
                expert_tile(0, 3, q)
            with act.Fori(1, TT - 1) as tt:
                load_scores(tt + 1)
                with act.Fori(0, 3) as i:
                    for q in range(4):
                        expert_tile(tt, i, q)
                for q in range(4):
                    if q == 1:
                        softmax(tt + 1)
                    expert_tile(tt, 3, q)
            with act.Fori(0, 3) as i:
                for q in range(4):
                    expert_tile(TT - 1, i, q)
            for q in range(4):
                expert_tile(TT - 1, 3, q)
            store_gates(NE - 1, T // TB - 1)

            def ple_out(ns):
                for n in ns:
                    s = n % 2
                    if n % 4 == 3:
                        act.wait_ge(tile_done, 2 * P_PAIR + n // 4 + 1)
                    else:
                        act.wait_ge(ple_filled, n - n // 4 + 1)
                    act.copy(ple[:, n, :], main[s][:, :]).then_inc(main_drained[s], 1)

            def load_act(b, k):
                act.dma_start(act_in_b[:, k, :], act_d[bass.ds(EG * b + k, 1)].rearrange("a p n -> p (a n)")) \
                    .then_inc(act_in[k], 16)

            def load_gates(b, blocks=slice(0, T // TB)):
                act.dma_start(gate_in[:, blocks, :, :].rearrange("p b e t -> p b (e t)"),
                              gate_d[blocks, :, bass.ds(EG * b, EG), :].rearrange("b p e t -> p b (e t)")) \
                    .then_inc(gate_ins, 16)

            act.copy(gate_in[:, T // TB - 1, :, :], gbuf[:, 0:EG, :]).then_inc(gate_ins, 16)
            for q in act_st:
                act.wait_ge(q, 16 + 16 * (NE // 2))
            load_act(0, 0)
            act.wait_ge(gate_st, 16 + 16 * (T // TB - 1))
            load_gates(0, slice(0, T // TB - 1))
            for k in range(1, EG):
                load_act(0, k)
            ple_out(range(DC))
            act.wait_ge(gate_st, 16 + 16 * (T // TB))

            def hi_of_round(b, last=False):
                for k in range(EG):
                    act.wait_ge(h32_ready, EG * b + k + 1)
                    act.wait_ge(b_filled, 16 * b + 8 * (k // 2) + 8)
                    act.copy(h_hi[:, k, :], act_in_b[:, k, :]).then_inc(hhi_ready, 1)
                    if last:
                        continue
                    if k == 0:
                        act.wait_ge(h32_ready, EG * b + EG)
                        load_gates(b + 1)
                    elif k % 2:
                        for q in (k - 1, k):
                            act.wait_ge(h_ready, EG * b + q + 1)
                            load_act(b + 1, q)

            with act.Fori(0, NE // EG - 1) as b:
                hi_of_round(b)
            hi_of_round(NE // EG - 1, last=True)

            for c in range(DC):
                act.wait_ge(b_drained[c % 4], 4 * (NE // EG) + c // 4)
                square(2 * DC + c, res[:, c, :])
            norm_std(NORM2, 2)
            hi_rows(a_hi, 2)
            with act.Fori(0, DC // 2) as i:
                for s in range(2):
                    act.wait_ge(tile_done, F_TILE + 2 * i + s + 1)
                    act.wait_ge(f_added, 2 * i + s + 1)
                    act.activation(fg[:, s, :], main[s][:, :], ACT.Sigmoid).then_inc(main_drained[s], 1)
                    act.wait_ge(f_added, 2 * i + s + 3)
                    act.wait_ge(sq_added, 3 * DC + 2 * i + s - 1)
                    act.activation(sqb[:, s, :], res[:, bass.ds(2 * i + s, 1), :].rearrange("p a t -> p (a t)"),
                                   ACT.Square).then_inc(sq_done, 1)
            norm_std(NORM3, 3)

        @block.vector
        def _(dve):
            steps = Steps(dve, dve_step)

            def add_square(i, first, s):
                dve.wait_ge(sq_done, i + 1)
                if first:
                    dve.tensor_copy(nt2[:, :], sqb[:, s, :]).then_inc(sq_added, 1)
                else:
                    dve.wait_ge(sq_added, i)
                    dve.tensor_tensor(nt2[:, :], nt2[:, :], sqb[:, s, :], ALU.add).then_inc(sq_added, 1)

            def newton(slot, rough, rough_done, drained, value):
                dve.wait_ge(rough, rough_done - 1)
                dve.tensor_scalar(nt1[:, :], slot[:, :], -0.5, -0.5 * EPS, ALU.mult, ALU.add).then_inc(drained, 1)
                dve.wait_ge(rough, rough_done)
                steps.then(dve.tensor_tensor(nt2[:, :], nt0[:, :], nt0[:, :], ALU.mult))
                dve.wait_ge(drained, value)
                steps.then(dve.tensor_tensor(nt2[:, :], nt2[:, :], nt1[:, :], ALU.mult))
                steps.then(dve.scalar_tensor_tensor(nt0[:, :], nt2[:, :], 1.5, nt0[:, :], ALU.add, ALU.mult))

            def norm_rstd(m, count):
                newton(scr[0], std_done, 2 * count + 2, scr_drained[0], m.drained("stat"))

            def norm_rows(norm, first, which, dst_lo, dst_hi):
                def row(c):
                    if c >= 4:
                        dve.wait_ge(norm_lo[c % 2], 4 * norm + c // 2 - 1)
                    dve.scalar_tensor_tensor(rowb[:, c % 4, :], res[:, c, :], gain[:, which, c:c + 1], nt0[:, :],
                                             ALU.mult, ALU.mult).then_inc(row_made, 1)
                row(0)
                row(1)
                for c in range(0, DC, 2):
                    if c + 2 < DC:
                        row(c + 2)
                    dve.wait_ge(row_hi, first + c + 1)
                    dve.tensor_tensor(dst_lo[:, c, :], rowb[:, c % 4, :], dst_hi[:, c, :].bitcast(F32),
                                      ALU.subtract).then_inc(norm_lo[0], 1)
                    if c + 3 < DC:
                        row(c + 3)
                dve.wait_ge(norm_lo[0], 4 * norm + 4)
                dve.wait_ge(norm_lo[1], 4 * norm + 4)

            dve.memset(ones_d[:, :], 1.0 / D).then_inc(ones_set, 1)
            dve.memset(ones_v[:, :], 1.0 / DV).then_inc(ones_set, 1)
            dve.memset(eps_t[:, :], EPS).then_inc(ones_set, 1)
            dve.sem_inc(ret_ready, 1)
            dve.sem_inc(merged_done, 1)
            dve.sem_inc(z_used, 1)
            dve.sem_inc(oh_hi_ready, 1)
            dve.sem_inc(oh_lo_ready, 1)
            dve.sem_inc(head_ranked, 1)
            dve.sem_inc(f_added, 2)
            for c in range(DC):
                add_square(c, c == 0, c % 2)
            norm_rstd(Scratch([("stat", 0)], 0, (0, 0)), 0)
            dve.wait_ge(consts_in, 16 * 5)
            norm_rows(0, 0, 0, a_lo, a_hi)
            dve.wait_ge(rope_in, 32)

            def rotary(dst, s):
                steps.mark(dve.tensor_tensor(dst[:, :], main[s][:, :], cos[:, :], ALU.mult))
                steps.mark(dve.tensor_copy(swapped[0:64, :], main[s][64:128, :]))
                dve.tensor_copy(swapped[64:128, :], main[s][0:64, :]).then_inc(main_drained[s], 1)

            def rotary_end(dst):
                steps.then(dve.tensor_tensor(swapped[:, :], swapped[:, :], sin[:, :], ALU.mult))
                dve.tensor_tensor(dst[:, :], dst[:, :], swapped[:, :], ALU.add).then_inc(kq_ready, 1)

            def lo_of(first, dst_lo, dst_hi, src, cs=range(DC)):
                for c in cs:
                    dve.wait_ge(row_hi, first + c + 1)
                    dve.tensor_tensor(dst_lo[:, c, :], src[:, c, :], dst_hi[:, c, :].bitcast(F32), ALU.subtract) \
                        .then_inc(row_lo, 1)

            def head(h, first=False, last=False):
                m = retention_scratch(h)
                if not last:
                    for s, dst in ((0, kT), (1, qT)):
                        dve.wait_ge(tile_done, 6 * h + s + 1)
                        if s and not first:
                            dve.wait_ge(scr_filled, m.filled("o1"))
                        if not (first and s == 0):
                            dve.wait_ge(kq_ready, 2 * h + s)
                        rotary(dst, s)
                        dve.wait_ge(dve_step, steps.n)
                        dve.wait_ge(main_drained[s], 3 * h + 2)
                        rotary_end(dst)
                if not first:
                    for e in range(2):
                        dve.wait_ge(scr_drained[e], m.drained(f"o{e}"))
                    dve.tensor_tensor(nt2[:, :], y[:, 0, :], y[:, 1, :], ALU.add).then_inc(ysum_ready, 1)
                    dve.wait_ge(scr_filled, m.filled("mean"))
                    for e in range(2):
                        dve.tensor_tensor(y[:, e, :], y[:, e, :], scr[0][:, :], ALU.subtract).then_inc(centered, 1)
                    dve.wait_ge(centered, 2 * h)
                    dve.sem_inc(scr_drained[0], 1)
                if last:
                    lo_of(DC, mix_lo, mix_hi, res, range(0, 1))
                if not last:
                    dve.wait_ge(scr_filled, m.filled("scores"))
                    dve.wait_ge(headc_in, 32 * h + 32)
                    dve.tensor_tensor(sdec[:, :, :], scr[0][:, :].rearrange("p (n i) -> p n i", n=NCH),
                                      headc[:, 0:CHUNK].unsqueeze(1).to_broadcast([P, NCH, CHUNK]),
                                      ALU.mult).then_inc(scr_drained[0], 1)
                    q3 = qT[:, :].rearrange("p (n i) -> p n i", n=NCH)
                    dve.wait_ge(kq_ready, 2 * h + 2)
                    dve.tensor_tensor(q3, q3, xi.unsqueeze(1).to_broadcast([P, NCH, CHUNK]), ALU.mult) \
                        .then_inc(qxi_ready, 1)
                if not first:
                    dve.wait_ge(ysq_ready, 2 * h)
                    dve.tensor_tensor(nt2[:, :], sqb[:, 0, :], sqb[:, 1, :], ALU.add).then_inc(ysqsum_ready, 1)
                    if last:
                        lo_of(DC, mix_lo, mix_hi, res, range(1, 4))
                    newton(scr[1], gstd_done, 2 * h, scr_drained[1], m.drained("var"))
                    for e in range(2):
                        steps.mark(dve.tensor_tensor(y[:, e, :], y[:, e, :], nt0[:, :], ALU.mult))
                    dve.wait_ge(dve_step, steps.n)
                    for e in range(2):
                        dve.tensor_tensor(res[:, bass.ds(2 * (h - 1) + e, 1), :].rearrange("p a t -> p (a t)")
                                          if not isinstance(h, int) else res[:, 2 * (h - 1) + e, :],
                                          y[:, e, :], g[:, e, :], ALU.mult).then_inc(ret_ready, 1)
                if not last:
                    for e in range(2):
                        dve.wait_ge(sig_ready, 2 * h + e + 1)
                        dve.tensor_tensor(g[:, e, :], g[:, e, :], main[e][:, :], ALU.mult) \
                            .then_inc(main_drained[e], 1)
                    for e, ns in ((0, range(0, 4)), (1, range(4, NCH - 1))):
                        dve.wait_ge(scr_filled, m.filled(f"kv{e}"))
                        for n in ns:
                            kv = scr[e][:, (n - 4 * e) * DV:(n - 4 * e + 1) * DV]
                            if n == 0:
                                ins = dve.tensor_copy(state[:, 0, :], kv)
                            else:
                                ins = dve.scalar_tensor_tensor(state[:, n, :], state[:, n - 1, :], headz[:, 1:2],
                                                               kv, ALU.mult, ALU.add)
                            if n == 3:
                                ins.then_inc(scr_drained[0], 1)
                                dve.wait_ge(scr_drained[0], m.drained("kv0"))
                            elif n == NCH - 2:
                                ins.then_inc(scr_drained[1], 1)
                                dve.wait_ge(scr_drained[1], m.drained("kv1"))
                                dve.sem_inc(states_ready, 1)
                            else:
                                steps.then(ins)

            head(0, first=True)
            with dve.Fori(1, HEADS) as h:
                inside = steps.enter(h - 1, 6 + 3 + 2 + 5)
                head(h)
                steps.leave(inside, HEADS - 1)
            head(HEADS, last=True)

            dve.wait_ge(ret_ready, 2 * HEADS + 1)
            lo_of(DC, mix_lo, mix_hi, res, range(4, DC))
            with dve.Fori(0, DC) as n:
                dve.wait_ge(main_drained[0], M1_PAIR + n + 2)
                dve.wait_ge(tile_done, 2 * (M1_PAIR + n) + 2)
                dve.tensor_tensor(res[:, bass.ds(n, 1), :].rearrange("p a t -> p (a t)"), main[1][:, :], sg[:, :],
                                  ALU.mult).then_inc(main_drained[1], 1)
                dve.wait_ge(main_drained[1], M1_PAIR + n + 2)
                dve.sem_inc(merged_done, 1)

            dve.memset(pbuf[:, 0:2], 0.0).then_inc(ones_set, 1)
            dve.wait_ge(ones_set, 4)
            with dve.Fori(0, DC // 2) as i:
                inside = steps.enter(i, 2 * 3)
                for k in range(2):
                    tiles = [3 * k, 3 * k + 1, 3 * k + 2]
                    s_ch, s_cb = tiles[1] % 2, tiles[2] % 2
                    pair_ch, pair_cb = C_PAIR + 3 * i + tiles[1] // 2, C_PAIR + 3 * i + tiles[2] // 2
                    j = 2 * i + k

                    def c_of(q):
                        return convc[:, bass.ds(j, 1), q:q + 1].rearrange("p a q -> p (a q)")

                    dve.wait_ge(main_drained[k], C_PAIR + 3 * i + tiles[0] // 2 + 2)
                    dve.wait_ge(tile_done, 2 * pair_ch + s_ch + 1)
                    dve.tensor_tensor(pbuf[:, 2:T + 2], main[s_ch][:, :], sg[:, :], ALU.mult) \
                        .then_inc(main_drained[s_ch], 1)
                    dve.wait_ge(main_drained[s_ch], pair_ch + 2)
                    dve.sem_inc(merged_done, 1)
                    dve.wait_ge(z_used, j + 1)
                    steps.then(dve.tensor_scalar(z[:, :], pbuf[:, 2:T + 2], c_of(2), c_of(3), ALU.mult, ALU.add))
                    steps.then(dve.scalar_tensor_tensor(z[:, :], pbuf[:, 1:T + 1], c_of(1), z[:, :],
                                                        ALU.mult, ALU.add))
                    steps.then(dve.scalar_tensor_tensor(z[:, :], pbuf[:, 0:T], c_of(0), z[:, :],
                                                        ALU.mult, ALU.add))
                    dve.wait_ge(tile_done, 2 * pair_cb + s_cb + 1)
                    dve.tensor_tensor(z[:, :], main[s_cb][:, :], z[:, :], ALU.mult).then_inc(main_drained[s_cb], 1)
                    dve.wait_ge(main_drained[s_cb], pair_cb + 2)
                    dve.sem_inc(z_ready, 1)
                    dve.wait_ge(z_hi, j + 1)
                    dve.tensor_tensor(mix_lo[:, bass.ds(j, 1), :].rearrange("p a t -> p (a t)"), z[:, :],
                                      mix_hi[:, bass.ds(j, 1), :].rearrange("p a t -> p (a t)").bitcast(F32),
                                      ALU.subtract).then_inc(z_used, 1)
                steps.leave(inside, DC // 2)
            def merge(n):
                r = res[:, bass.ds(n, 1), :].rearrange("p a t -> p (a t)")
                dve.wait_ge(main_drained[0], M2_PAIR + n + 2)
                dve.wait_ge(tile_done, 2 * (M2_PAIR + n) + 2)
                dve.tensor_tensor(sg[:, :], main[1][:, :], sg[:, :], ALU.mult).then_inc(main_drained[1], 1)
                dve.wait_ge(main_drained[1], M2_PAIR + n + 2)
                steps.then(dve.tensor_tensor(r, r, sg[:, :], ALU.add))
                dve.sem_inc(merged_done, 1)

            with dve.Fori(0, DC - 1) as n:
                inside = steps.enter(n, 1)
                merge(n)
                steps.leave(inside, DC - 1)
            dve.wait_ge(tile_done, 2 * (M2_PAIR + DC - 1) + 1)
            lo_of(2 * DC, a_lo, a_hi, res, range(DC - 1))
            merge(DC - 1)
            lo_of(2 * DC, a_lo, a_hi, res, range(DC - 1, DC))
            steps.then(dve.memset(nt2[:, :], 0.0))
            for c in range(DC):
                dve.wait_ge(x_in[c], 32)
            with dve.Fori(0, DC // 2) as i:
                for s in range(2):
                    r = res[:, bass.ds(2 * i + s, 1), :].rearrange("p a t -> p (a t)")
                    dve.wait_ge(tile_done, 2 * (O_PAIR + i) + s + 1)
                    dve.tensor_tensor(r, main[s][:, :], r, ALU.add).then_inc(main_drained[s], 1)
                    if s == 0:
                        dve.wait_ge(sq_done, DC + 2 * i + 1)
                        dve.wait_ge(sq_added, DC + 2 * i)
                    else:
                        dve.wait_ge(sq_done, DC + 2 * i + 2)
                        dve.wait_ge(sq_added, DC + 2 * i + 1)
                    dve.tensor_tensor(nt2[:, :], nt2[:, :], sqb[:, s, :], ALU.add).then_inc(sq_added, 1)
            norm_rstd(NORM1, 1)
            norm_rows(1, 3 * DC, 1, mix_lo, mix_hi)
            for c in range(2):
                dve.wait_ge(row_hi, 4 * DC + c + 1)
                dve.tensor_tensor(p_lo[:, c, :], p_raw[:, :], p_hi[:, c, :].bitcast(F32), ALU.subtract) \
                    .then_inc(row_lo, 1)

            def settled():
                dve.wait_ge(dve_step, steps.n)
                dve.sem_inc(passed, 1)

            def rank(s1, s2, h):
                src = (s1, s2)
                settled()
                for s in range(2):
                    steps.mark(dve.max(v16[:, s, 0:8], src[s]))
                settled()
                for s in range(2):
                    steps.mark(dve.max_index(ix[:, s, 0:8], v16[:, s, 0:8], src[s]))
                    steps.mark(dve.match_replace(left[:, s, :], v16[:, s, 0:8], src[s], LOWEST))
                settled()
                for s in range(2):
                    steps.mark(dve.max(v16[:, s, 8:16], left[:, s, :]))
                settled()
                for s in range(2):
                    steps.mark(dve.max_index(ix[:, s, 8:16], v16[:, s, 8:16], left[:, s, :]))
                settled()
                steps.mark(dve.tensor_tensor(cand[:, :, :], v16[:, 0, :].unsqueeze(2).to_broadcast([P, TOPK, TOPK]),
                                             v16[:, 1, :].unsqueeze(1).to_broadcast([P, TOPK, TOPK]), ALU.add))
                flat = cand[:, :, :].rearrange("p a b -> p (a b)")
                settled()
                steps.mark(dve.max(top[:, 0:8], flat))
                settled()
                steps.mark(dve.max_index(ix[:, 2, 0:8], top[:, 0:8], flat))
                steps.mark(dve.match_replace(candl, top[:, 0:8], flat, LOWEST))
                settled()
                steps.mark(dve.max(top[:, 8:16], candl))
                settled()
                steps.mark(dve.max_index(ix[:, 2, 8:16], top[:, 8:16], candl))
                settled()
                steps.mark(dve.tensor_copy(sel_ix[:, bass.ds(h, 1), :].rearrange("p a k -> p (a k)"),
                                           ix[:, :, :].rearrange("p a k -> p (a k)")))
                steps.mark(dve.tensor_copy(sel_v[:, bass.ds(h, 1), :].rearrange("p a k -> p (a k)"), top[:, :]))
                settled()
                dve.sem_inc(head_ranked, 1)

            RANK = 18

            def pick_begin(tt):
                steps.then(dve.tensor_copy(gsum[:, :], sel_v[:, :, 0:1].rearrange("p h a -> p (h a)")))
                steps.then(dve.tensor_tensor(sel_v[:, :, :], sel_v[:, :, :],
                                             gsum[:, :].unsqueeze(2).to_broadcast([P, PH, TOPK]), ALU.subtract))
                dve.sem_inc(tops_ready, 1)
                pos = sel_ix[:, :, 2 * TOPK:3 * TOPK]
                steps.mark(dve.tensor_scalar(pos_a[:, :, :], pos, 4, None, ALU.logical_shift_right))
                steps.then(dve.tensor_scalar(pos_b[:, :, :], pos, TOPK - 1, None, ALU.bitwise_and))

            def pick_keys(pairs):
                eq4 = eq[:, :, :].rearrange("p (h k) a -> p h k a", h=PH)
                for which, at in pairs:
                    steps.then(dve.tensor_tensor(
                        eq[:, :, :],
                        at[:, :, :].rearrange("p h k -> p (h k)").unsqueeze(2).to_broadcast([P, PH * TOPK, TOPK]),
                        iota16[:, :].unsqueeze(1).to_broadcast([P, PH * TOPK, TOPK]), ALU.is_equal))
                    steps.then(dve.tensor_tensor(
                        eq4, eq4,
                        sel_ix[:, :, which * TOPK:(which + 1) * TOPK].unsqueeze(2)
                        .to_broadcast([P, PH, TOPK, TOPK]), ALU.mult))
                    steps.then(dve.tensor_reduce(picked[:, which, :], eq[:, :, :], AX_X, ALU.add))

            def pick_end(tt):
                dve.wait_ge(exp_done, tt + 1)
                steps.then(dve.tensor_reduce(gsum[:, :], sel_v[:, :, :], AX_X, ALU.add))
                steps.then(dve.reciprocal(gsum[:, :], gsum[:, :]))
                steps.then(dve.tensor_tensor(picked[:, 2, :].rearrange("p (h k) -> p h k", h=PH), sel_v[:, :, :],
                                             gsum[:, :].unsqueeze(2).to_broadcast([P, PH, TOPK]), ALU.mult))
                dve.sem_inc(picked_ready, 1)

            PICK = 13

            with dve.Fori(0, PH) as h:
                inside = steps.enter(h, RANK)
                m = query_scratch(h)
                for s in range(2):
                    dve.wait_ge(scr_drained[s], m.drained(f"s{s}"))
                rank(stage[:, 0, 0:P], stage[:, 1, 0:P], h)
                steps.leave(inside, PH)
            pick_begin(0)
            pick_keys(((0, pos_a), (1, pos_b)))
            pick_end(0)

            def onehots(m, mq):
                for w in range(2):
                    cols = slice(8 * mq + 4 * w, 8 * mq + 4 * w + 4)
                    dve.wait_ge(gates_filled, 2 * m + w + 1)
                    dve.tensor_tensor(hot[:, w, :, :, :], iota[:, :].unsqueeze(1).unsqueeze(1)
                                      .to_broadcast([P, 2, 4, NKEYS]),
                                      few[:, 0:2, cols].unsqueeze(3).to_broadcast([P, 2, 4, NKEYS]),
                                      ALU.is_equal).then_inc(hot_made, 1)
                    dve.wait_ge(hot_made, 2 * m + w + 1)
                    dve.tensor_tensor(oh1[:, 4 * w:4 * w + 4, 1, :], hot[:, w, 0, :, :].bitcast(F32),
                                      few[:, 3, cols].unsqueeze(2).to_broadcast([P, 4, NKEYS]),
                                      ALU.mult).then_inc(oh_lo_ready, 1)

            def gates_out(m, mq, block):
                for w in range(2):
                    dve.wait_ge(gates_filled, 2 * m + w + 3)
                    if mq == 0 and w == 0:
                        dve.wait_ge(gate_st, 16 * block + 16)
                    dve.tensor_reduce(gbuf[:, :, 8 * mq + 4 * w:8 * mq + 4 * w + 4].rearrange("p e t -> p t e"),
                                      scr[w][:, :].rearrange("p (t a e) -> p t e a", t=4, a=2), AX_X, ALU.add) \
                        .then_inc(gates_drained, 1)

            def turn(tt, i, first, between, start=False):
                if first:
                    m = select_scratch(tt)
                    dve.wait_ge(scr_filled, m.filled("sel"))
                    dve.wait_ge(oh_hi_ready, 32 * tt + 1)
                    dve.tensor_copy(packed[:, 0:3, :].rearrange("p a t -> p (a t)"), scr[1][:, 0:3 * P]) \
                        .then_inc(scr_drained[1], 1)
                    dve.wait_ge(scr_drained[1], m.drained("sel"))
                    steps.then(dve.tensor_copy(gate_r[:, :], packed[:, 2, :]))
                    steps.then(dve.tensor_tensor(packed[:, 3, :], packed[:, 2, :], gate_r[:, :].bitcast(F32),
                                                 ALU.subtract))
                    steps.then(dve.tensor_copy(packed[:, 2, :], gate_r[:, :].bitcast(F32)))
                for q in range(4):
                    if not (start and q == 0):
                        gates_out(16 * tt + 4 * i + q - 1, (q - 1) % 4, 4 * tt + i - (q == 0))
                    if q == 0:
                        dve.wait_ge(oh_lo_ready, 32 * tt + 8 * i + 1)
                        dve.wait_ge(oh_hi_ready, 32 * tt + 8 * i + 1)
                        steps.then(dve.tensor_copy(few[:, :, :], packed[:, :, bass.ds(TB * i, TB)]))
                    onehots(16 * tt + 4 * i + q, q)
                    between(q)

            def rank_next(h):
                steps.then(dve.tensor_copy(pair_s[:, :, :], scores[:, bass.ds(2 * h, 2), :]))
                rank(pair_s[:, 0, :], pair_s[:, 1, :], h)

            def nothing(q):
                pass

            def token_tile(tt, start=False):
                def first_heads(q):
                    if q == 1 and not start:
                        dve.wait_ge(score_in, 16 * tt + 16)
                        rank_next(0)
                    elif q == (0 if start else 2):
                        rank_next(1)

                if start:
                    dve.wait_ge(score_in, 16 * tt + 16)
                    rank_next(0)

                turn(tt, 0, True, first_heads, start)
                with dve.Fori(1, 3) as i:
                    inner = steps.enter(i - 1, 1 + 3 * (1 + RANK))
                    turn(tt, i, False, lambda q: rank_next(3 * i - 1 + q) if q < 3 else None)
                    steps.leave(inner, 2)

                def pick_next(q):
                    if q == 0:
                        pick_begin(tt + 1)
                        pick_keys(((0, pos_a),))
                    elif q == 1:
                        pick_keys(((1, pos_b),))
                    elif q == 2:
                        pick_end(tt + 1)

                turn(tt, 3, False, pick_next)

            token_tile(0, True)
            with dve.Fori(1, TT - 1) as tt:
                outer = steps.enter(tt - 1, 3 + 4 + PH * (1 + RANK) + PICK)
                token_tile(tt)
                steps.leave(outer, TT - 2)
            turn(TT - 1, 0, True, nothing)
            with dve.Fori(1, 4) as i:
                inner = steps.enter(i - 1, 1)
                turn(TT - 1, i, False, nothing)
                steps.leave(inner, 3)
            gates_out(NE - 1, 3, T // TB - 1)

            def weigh(b):
                dve.wait_ge(gate_ins, 16 * b + 32)
                for k in range(EG):
                    rows = act_in_b[:, k, :].rearrange("p (b t) -> p b t", t=TB)
                    dve.wait_ge(act_in[k], 16 * b + 16)
                    dve.tensor_tensor(rows, rows, gate_in[:, :, k, :], ALU.mult).then_inc(h32_ready, 1)

            def lo_of_round(b, ks):
                for k in ks:
                    dve.wait_ge(hhi_ready, EG * b + k + 1)
                    dve.tensor_tensor(h_lo[:, k, :], act_in_b[:, k, :], h_hi[:, k, :].bitcast(F32), ALU.subtract) \
                        .then_inc(h_ready, 1)

            def sums(b, e, square_of=None):
                for dt in range(DC):
                    dve.wait_ge(b_filled, 16 + 16 * b + 8 * e + dt + 1)
                    dve.wait_ge(b_drained[dt % 4], 4 * b + 2 * e + dt // 4 + 1)
                    dve.tensor_tensor(res[:, dt, :], bslot[dt % 4][:, :], res[:, dt, :], ALU.add) \
                        .then_inc(b_drained[dt % 4], 1)
                    if square_of is not None and dt:
                        square_of(dt - 1)

            weigh(0)
            lo_of_round(0, range(EG))
            with dve.Fori(0, NE // EG - 1) as b:
                sums(b, 0)
                weigh(b + 1)
                lo_of_round(b + 1, (0, 1))
                sums(b, 1)
                lo_of_round(b + 1, (2, 3))
            sums(NE // EG - 1, 0)
            sums(NE // EG - 1, 1, square_of=lambda c: add_square(2 * DC + c, c == 0, c % 2))
            add_square(3 * DC - 1, False, 1)
            norm_rstd(NORM2, 2)
            norm_rows(2, 4 * DC + 2, 2, a_lo, a_hi)
            steps.then(dve.memset(nt2[:, :], 0.0))
            with dve.Fori(0, DC // 2) as i:
                inside = steps.enter(i, 2)
                for s in range(2):
                    r = res[:, bass.ds(2 * i + s, 1), :].rearrange("p a t -> p (a t)")
                    pl = ple[:, bass.ds(2 * i + s, 1), :].rearrange("p a t -> p (a t)")
                    dve.wait_ge(main_drained[s], F_MAIN + i + 2)
                    steps.then(dve.tensor_tensor(fg[:, s, :], fg[:, s, :], pl, ALU.mult))
                    dve.tensor_tensor(r, r, fg[:, s, :], ALU.add).then_inc(f_added, 1)
                    dve.wait_ge(sq_done, 3 * DC + 2 * i + s + 1)
                    dve.wait_ge(sq_added, 3 * DC + 2 * i + s)
                    dve.tensor_tensor(nt2[:, :], nt2[:, :], sqb[:, s, :], ALU.add).then_inc(sq_added, 1)
                steps.leave(inside, DC // 2)
            norm_rstd(NORM3, 3)
            for c in range(DC):
                dve.scalar_tensor_tensor(res[:, c, :], res[:, c, :], gain[:, 3, c:c + 1], nt0[:, :],
                                         ALU.mult, ALU.mult).then_inc(out_ready, 1)


def weight_tiles(w):
    k, n = w.shape
    return w.reshape(k // P, P, n // P, P).transpose(2, 1, 0, 3).reshape(n // P, P, k)


def shape_constants():
    f = np.float32
    half = DK // 2
    inv = (f(10000.0) ** (-np.arange(half, dtype=f) / f(half))).astype(f)
    ang = (np.arange(T, dtype=f)[None, :] * inv[:, None]).astype(f)
    cos, sin = np.cos(ang).astype(f), np.sin(ang).astype(f)
    rope = np.stack([np.concatenate([cos, cos]), np.concatenate([-sin, sin])])
    scale = f(DK) ** f(-0.5)
    log_gamma = np.log1p(-(f(2.0) ** (f(-5.0) - np.arange(HEADS, dtype=f)))).astype(f)
    pos = np.arange(CHUNK, dtype=f)
    diff = pos[None, :] - pos[:, None]
    head = np.zeros((HEADS, P, 2 * CHUNK + 2), f)
    for h in range(HEADS):
        lg = log_gamma[h]
        head[h, :, 0:CHUNK] = np.where(diff >= 0, np.exp(lg * np.where(diff >= 0, diff, f(0))), f(0)) * scale
        head[h, :, CHUNK:2 * CHUNK] = np.exp(lg * (pos + f(1)))[None, :]
        head[h, :, 2 * CHUNK] = np.exp(lg * (f(CHUNK - 1) - pos)) * scale
        head[h, :, 2 * CHUNK + 1] = np.exp(lg * f(CHUNK))
    shape_c = np.stack([np.eye(P, dtype=f), np.broadcast_to(np.arange(P, dtype=f), (P, P))])
    return rope, head, np.ascontiguousarray(shape_c)


def kernel(x, p, g_mix, w_in, conv_w, conv_b, w_ret_up, w_conv_up, w_out, g_ffn, w_peer_q, peer_k1,
           peer_k2, peer_u, peer_v, g_ple, w_ple_proj, w_ple_gate, g_final):
    import concourse.bacc as bacc
    from concourse.bass_utils import run_bass_kernel_spmd

    def a(v):
        return np.asarray(v)

    w_in_t = weight_tiles(a(w_in)[0])
    at = np.cumsum([0, 4, 4, 8, 8, 8, 8, 8, 8, 8])
    q_, k_, v_, g_, cb, cc, ch, gr, gc = [w_in_t[at[i]:at[i + 1]] for i in range(9)]
    up_r, up_c, w_o = (weight_tiles(a(w)[0]) for w in (w_ret_up, w_conv_up, w_out))
    parts = []
    for h in range(HEADS):
        parts += [k_[h], q_[h], v_[2 * h], v_[2 * h + 1], g_[2 * h], g_[2 * h + 1]]
    for n in range(DC):
        parts += [gr[n], up_r[n]]
    for j in range(DC):
        parts += [cc[j], ch[j], cb[j]]
    for n in range(DC):
        parts += [gc[n], up_c[n]]
    u_tiles = a(peer_u)[0].reshape(NE, P, DC, P).transpose(0, 3, 2, 1).reshape(NE, P, D)
    ple_tiles = weight_tiles(a(w_ple_proj)[0]).reshape(2, 4, P, PLE).transpose(0, 2, 1, 3).reshape(2, P, D)
    stream = np.concatenate([
        np.stack(parts), w_o, weight_tiles(a(w_peer_q)[0]), u_tiles, ple_tiles,
        a(peer_v)[0].reshape(NE, P, D), weight_tiles(a(w_ple_gate)[0])])
    assert stream.shape[0] == 2 * PAIRS
    keys = np.stack([a(peer_k1)[0], a(peer_k2)[0]], 1)
    rope, head_c, shape_c = shape_constants()
    arrays = {
        "x_t": a(x)[0].T,
        "p_t": a(p)[0, 0].T,
        "stream": stream,
        "key_t": keys.transpose(3, 0, 1, 2).reshape(P, 2 * PH, NKEYS),
        "gains": np.stack([a(v).reshape(DC, P) for v in (g_mix, g_ffn, g_ple, g_final)]).transpose(2, 0, 1),
        "conv_c": np.concatenate([a(conv_w)[0], a(conv_b)]).reshape(4, DC, P).transpose(2, 1, 0),
        "rope": rope, "head_c": head_c, "shape_c": shape_c,
    }
    arrays = {k: np.ascontiguousarray(v) for k, v in arrays.items()}
    nc = bacc.Bacc("TRN2", target_bir_lowering=False, num_devices=1)
    ins = [nc.dram_tensor(k, v.shape, F32, kind="ExternalInput").ap() for k, v in arrays.items()]
    out_t = nc.dram_tensor("out_t", (D, T), F32, kind="ExternalOutput").ap()
    score_d = nc.dram_tensor("score_d", (TT, P, 2 * PH, NKEYS), F32, kind="Internal").ap()
    act_d = nc.dram_tensor("act_d", (NE, P, T), F32, kind="Internal").ap()
    gate_d = nc.dram_tensor("gate_d", (T // TB, P, NKEYS, TB), F32, kind="Internal").ap()
    build(nc, *ins, out_t, score_d, act_d, gate_d)
    r = run_bass_kernel_spmd(nc, [arrays], core_ids=[0])
    return np.ascontiguousarray(r.results[0]["out_t"].T)[None]
```
